# Optimizing a Trainium2 kernel written in Bass

```python
import jax, jax.numpy as jnp
from jax import lax
import numpy as np

D_MODEL = 2048
BATCH = 1
SEQ = 512
DEPTH = 2

N_META = 16
BLOCK = 128
PAD_FRONT = BLOCK - N_META
REAL_START = BLOCK
RMS_EPS = 1e-6
NEG_INF = -1e30
LOG_FLOOR = 1e-30

HA = 4
DK_A = 128
DV_A = 128
A_WIDTH = HA * DV_A
CHUNK_A = 16

HB = 16
KVH_B = 2
DH_B = 64
B_WIDTH = HB * DH_B
WINDOW = 128
ROPE_THETA = 10000.0

POOL_WINDOWS = (2, 4, 8, 16)
NG_C = 4
CG_C = 128
C_WIDTH = NG_C * CG_C

MIX_WIDTH = A_WIDTH + B_WIDTH + C_WIDTH
IN_SIZES = (HA * DK_A, HA * DK_A, A_WIDTH, A_WIDTH,
            B_WIDTH, KVH_B * DH_B, KVH_B * DH_B, B_WIDTH,
            C_WIDTH, C_WIDTH)
IN_COLS = sum(IN_SIZES)

kernel_name = "hymba_hgrn2_swa_pool_hybrid"

def rms_norm(x, g):
    x32 = x.astype(jnp.float32)
    y = x32 * lax.rsqrt(jnp.mean(x32 * x32, axis=-1, keepdims=True) + RMS_EPS)
    return (y * g.astype(jnp.float32)).astype(x.dtype)

def rope(x, pos):
    d = x.shape[-1]
    half = d // 2
    inv = jnp.power(ROPE_THETA, -jnp.arange(half, dtype=jnp.float32) * 2.0 / d)
    ang = pos.astype(jnp.float32)[:, None] * inv[None, :]
    cos = jnp.cos(ang)[None, :, None, :]
    sin = jnp.sin(ang)[None, :, None, :]
    x32 = x.astype(jnp.float32)
    x1, x2 = x32[..., :half], x32[..., half:]
    out = jnp.concatenate([x1 * cos - x2 * sin, x2 * cos + x1 * sin], axis=-1)
    return out.astype(x.dtype)

def hgrn2_mixer(q, z_f, i_in, lb, valid):
    b, p = q.shape[0], q.shape[1]
    n = p // CHUNK_A
    lb32 = lb.astype(jnp.float32)
    z = z_f.astype(jnp.float32)
    m = valid[None, :, None]
    sig = jax.nn.sigmoid(z)
    f = lb32 + (1.0 - lb32) * sig
    log_f = jnp.log(jnp.maximum(f, LOG_FLOOR)) * m
    k = (1.0 - lb32) * (1.0 - sig) * m
    qf = jax.nn.silu(q.astype(jnp.float32))
    v = i_in.astype(jnp.float32)

    def heads(t, d):
        return t.reshape(b, n, CHUNK_A, HA, d).transpose(0, 3, 1, 2, 4)

    qf, k, log_f, v = heads(qf, DK_A), heads(k, DK_A), heads(log_f, DK_A), heads(v, DV_A)
    G = jnp.cumsum(log_f, axis=3)
    G_last = G[:, :, :, -1:, :]

    causal = jnp.tril(jnp.ones((CHUNK_A, CHUNK_A), dtype=bool))
    diff = G[:, :, :, :, None, :] - G[:, :, :, None, :, :]
    decay = jnp.exp(jnp.where(causal[:, :, None], diff, NEG_INF))
    attn = jnp.einsum('bhnik,bhnijk->bhnij', qf, decay * k[:, :, :, None, :, :])
    o_intra = jnp.einsum('bhnij,bhnjv->bhniv', attn, v)

    q_dec = qf * jnp.exp(G)
    k_dec = k * jnp.exp(G_last - G)
    a = jnp.exp(G_last[:, :, :, 0, :])

    def step(S, xs):
        qn, kn, vn, an = xs
        o = jnp.einsum('bhck,bhkv->bhcv', qn, S)
        S = an[..., None] * S + jnp.einsum('bhck,bhcv->bhkv', kn, vn)
        return S, o

    xs = (jnp.moveaxis(q_dec, 2, 0), jnp.moveaxis(k_dec, 2, 0),
          jnp.moveaxis(v, 2, 0), jnp.moveaxis(a, 2, 0))
    S0 = jnp.zeros((b, HA, DK_A, DV_A), jnp.float32)
    _, o_inter = lax.scan(step, S0, xs)
    return o_intra + jnp.moveaxis(o_inter, 0, 2)

def swa_sink_attention(q, k, v, sinks):
    b, p = q.shape[0], q.shape[1]
    nb = p // BLOCK
    grp = HB // KVH_B
    qb = q.reshape(b, nb, BLOCK, KVH_B, grp, DH_B)

    def band(t):
        tb = t.reshape(b, nb, BLOCK, KVH_B, DH_B)
        prev = jnp.pad(tb, ((0, 0), (1, 0), (0, 0), (0, 0), (0, 0)))[:, :nb]
        meta = jnp.broadcast_to(t[:, None, PAD_FRONT:REAL_START], (b, nb, N_META, KVH_B, DH_B))
        return jnp.concatenate([meta, prev, tb], axis=2)

    k_all, v_all = band(k), band(v)
    s = jnp.einsum('bnqkgd,bnskd->bnkgqs', qb, k_all).astype(jnp.float32) * (DH_B ** -0.5)

    q_idx = jnp.arange(nb)[:, None] * BLOCK + jnp.arange(BLOCK)[None, :]
    band_idx = jnp.arange(nb)[:, None] * BLOCK - BLOCK + jnp.arange(2 * BLOCK)[None, :]
    meta_idx = jnp.broadcast_to(PAD_FRONT + jnp.arange(N_META)[None, :], (nb, N_META))
    key_idx = jnp.concatenate([meta_idx, band_idx], axis=1)
    is_meta = jnp.concatenate([jnp.ones((N_META,), bool), jnp.zeros((2 * BLOCK,), bool)])
    qi = q_idx[:, :, None]
    kj = key_idx[:, None, :]
    in_band = (kj > qi - WINDOW) & (kj >= REAL_START)
    allowed = (kj <= qi) & (is_meta[None, None, :] | in_band)
    s = jnp.where(allowed[None, :, None, None], s, NEG_INF)

    sink = sinks.astype(jnp.float32).reshape(KVH_B, grp)[None, None, :, :, None, None]
    mx = jnp.maximum(jnp.max(s, axis=-1, keepdims=True), sink)
    pr = jnp.exp(s - mx)
    denom = jnp.sum(pr, axis=-1, keepdims=True) + jnp.exp(sink - mx)
    w = (pr / denom).astype(v.dtype)
    o = jnp.einsum('bnkgqs,bnskd->bnqkgd', w, v_all)
    return o.reshape(b, p, HB * DH_B)

def multiscale_pool(u, valid, pool_w, pool_scale):
    b, p = u.shape[0], u.shape[1]
    ug = (u.astype(jnp.float32) * valid[None, :, None]).reshape(b, p, NG_C, CG_C)
    cs = jnp.cumsum(ug, axis=1)
    cnt = jnp.cumsum(valid)
    outs = []
    for g, w in enumerate(POOL_WINDOWS):
        cs_g = cs[:, :, g]
        cs_prev = jnp.pad(cs_g, ((0, 0), (w, 0), (0, 0)))[:, :p]
        cnt_prev = jnp.pad(cnt, (w, 0))[:p]
        mean = (cs_g - cs_prev) / jnp.maximum(cnt - cnt_prev, 1.0)[None, :, None]
        outs.append((mean - ug[:, :, g]) * valid[None, :, None])
    pooled = jnp.stack(outs, axis=2)
    y = jnp.einsum('bpgc,gcd->bpgd', pooled, pool_w.astype(jnp.float32))
    return (y.reshape(b, p, C_WIDTH) * pool_scale.astype(jnp.float32)).astype(u.dtype)

def hybrid_layer(h, norm_g, w_in, lb, q_norm_g, k_norm_g, sinks, hgrn_norm_g,
                 pool_w, pool_scale, w_out, pos, valid):
    b, p = h.shape[0], h.shape[1]
    xn = rms_norm(h, norm_g)
    proj = xn @ w_in
    splits = np.cumsum(IN_SIZES)[:-1].tolist()
    qa, fa, ia, ga, qb, kb, vb, gb, uc, gc = jnp.split(proj, splits, axis=-1)

    oa = hgrn2_mixer(qa, fa, ia, lb, valid)
    oa = oa.transpose(0, 2, 3, 1, 4).reshape(b, p, HA, DV_A)
    ya = rms_norm(oa, hgrn_norm_g).reshape(b, p, A_WIDTH).astype(h.dtype)

    qh = rope(rms_norm(qb.reshape(b, p, HB, DH_B), q_norm_g), pos)
    kh = rope(rms_norm(kb.reshape(b, p, KVH_B, DH_B), k_norm_g), pos)
    vh = vb.reshape(b, p, KVH_B, DH_B)
    yb = swa_sink_attention(qh, kh, vh, sinks).astype(h.dtype)

    yc = multiscale_pool(uc, valid, pool_w, pool_scale)

    mixed = jnp.concatenate([ya * jax.nn.silu(ga), yb * jax.nn.silu(gb),
                             yc * jax.nn.silu(gc)], axis=-1)
    return h + mixed @ w_out

def setup_inputs(seed: int = 0) -> dict:
    key = jax.random.key(seed)
    ks = jax.random.split(key, 12)
    f32 = jnp.float32
    return {
        "x": jax.random.normal(ks[0], (BATCH, SEQ, D_MODEL), f32),
        "meta_tokens": jax.random.normal(ks[1], (N_META, D_MODEL), f32),
        "lb_logits": 0.5 * jax.random.normal(ks[2], (DEPTH, HA * DK_A), f32),
        "norm_g": 1.0 + 0.02 * jax.random.normal(ks[3], (DEPTH, D_MODEL), f32),
        "w_in": jax.random.normal(ks[4], (DEPTH, D_MODEL, IN_COLS), f32) * D_MODEL ** -0.5,
        "q_norm_g": 1.0 + 0.02 * jax.random.normal(ks[5], (DEPTH, DH_B), f32),
        "k_norm_g": 1.0 + 0.02 * jax.random.normal(ks[6], (DEPTH, DH_B), f32),
        "attn_sinks": 0.5 * jax.random.normal(ks[7], (DEPTH, HB), f32),
        "hgrn_norm_g": 1.0 + 0.02 * jax.random.normal(ks[8], (DEPTH, DV_A), f32),
        "pool_w": jax.random.normal(ks[9], (DEPTH, NG_C, CG_C, CG_C), f32) * CG_C ** -0.5,
        "pool_scale": 1.0 + 0.02 * jax.random.normal(ks[10], (DEPTH, C_WIDTH), f32),
        "w_out": jax.random.normal(ks[11], (DEPTH, MIX_WIDTH, D_MODEL), f32) * MIX_WIDTH ** -0.5,
    }

def reference(x, meta_tokens, lb_logits, norm_g, w_in, q_norm_g, k_norm_g, attn_sinks,
              hgrn_norm_g, pool_w, pool_scale, w_out):
    b = x.shape[0]
    h = jnp.concatenate([
        jnp.zeros((b, PAD_FRONT, D_MODEL), x.dtype),
        jnp.broadcast_to(meta_tokens.astype(x.dtype)[None], (b, N_META, D_MODEL)),
        x], axis=1)
    p = h.shape[1]
    idx = jnp.arange(p)
    valid = (idx >= PAD_FRONT).astype(jnp.float32)
    pos = idx - PAD_FRONT

    sm = jax.nn.softmax(lb_logits.astype(jnp.float32), axis=0)
    lb_all = jnp.cumsum(sm, axis=0) - sm[0:1]

    for l in range(DEPTH):
        h = hybrid_layer(h, norm_g[l], w_in[l], lb_all[l], q_norm_g[l], k_norm_g[l],
                         attn_sinks[l], hgrn_norm_g[l], pool_w[l], pool_scale[l],
                         w_out[l], pos, valid)
    return h[:, REAL_START:]


_drawn_inputs = setup_inputs


def setup_inputs(seed=0):
    import zlib

    import numpy as np

    out = dict(_drawn_inputs(seed))
    spreads = {}
    factors = {'lb_logits': 3.598,
     'norm_g': 3.665,
     'q_norm_g': 8.0,
     'k_norm_g': 8.0,
     'attn_sinks': 8.0,
     'hgrn_norm_g': 7.446,
     'pool_scale': 8.0}
    for name, (base, spread) in spreads.items():
        noise = np.random.default_rng([zlib.crc32(name.encode()), seed]).standard_normal(out[name].shape)
        drawn = base * np.exp(spread * noise) if base else spread * noise
        out[name] = __import__('jax').numpy.asarray(drawn.astype(out[name].dtype))
    for name, factor in factors.items():
        out[name] = (out[name] * factor).astype(out[name].dtype)
    return out
```

```python
from contextlib import ExitStack

import numpy as np

import concourse.bass as bass
from concourse import mybir

F32 = mybir.dt.float32
F32R = mybir.dt.float32r
U8 = mybir.dt.uint8
ACT = mybir.ActivationFunctionType
ALU = mybir.AluOpType

P = 128
DEPTH = 2
D_MODEL = 2048
N_META = 16
SEQ = 512
T = N_META + SEQ
KC = D_MODEL // P
HA = 4
HB = 16
DH = 64
GRP = 8
NG = 4
WINDOWS = (2, 4, 8, 16)
NBLK = SEQ // P
EPS = 1e-6
LOG_FLOOR = 1e-30
NEG = -1e30
PAD = 16

IN_CHUNKS = ([("k", 0), ("v", 0)] + [("q", i) for i in range(8)] + [("u", g) for g in range(NG)]
             + [("gate", 12 + g) for g in range(NG)]
             + [(kind, h) for h in range(HA) for kind in ("hf", "hq", "hi")]
             + [("gate", m) for m in (8, 9, 10, 11, 4, 5, 6, 7, 0, 1, 2, 3)])
N_IN = len(IN_CHUNKS)
CHUNKS = IN_CHUNKS + [("out", c) for c in range(KC)]
NC = len(CHUNKS)
NTOT = DEPTH * NC
GATES = [m for kind, m in IN_CHUNKS if kind == "gate"]
TICKS = KC

MINI = {0: ("rms", 0), 1: ("rope", 0)}
MINI.update({3 + i: ("rope", 1 + i) for i in range(8)})
MINI.update({11 + g: ("pool", g) for g in range(NG)})
MINI.update({22 + 3 * h: ("hnorm", h) for h in range(HA)})
MINI_SLOTS = sorted(MINI)
NORM_SLOTS = [n for n in MINI_SLOTS if MINI[n][0] != "pool"]
MINI_TICK = 8

ROPE_CHUNKS = [0] + list(range(2, 10))
NROPE = len(ROPE_CHUNKS)
TANH_CHUNKS = [n for n, (kind, _) in enumerate(IN_CHUNKS) if kind in ("gate", "hq")]

C_NORM, C_QG, C_QGS, C_KG, C_KGS, C_HG, C_PS, C_LB, C_SINK, NPRM = 0, 16, 17, 18, 19, 20, 21, 25, 33, 49

ATT_SLOT, ATT_TICK = 11, 2


def att_batches(layer):
    first = 0 if layer == 0 else 1
    return [(b, j, kv) for b in range(first, NBLK + 1) for j in range(2) for kv in range(2)]


def att_items(batch):
    return [4] if batch[0] == 0 else [0, 1, 2, 3, 4]


ATT_B = [att_batches(l) for l in range(DEPTH)]
ATT_Q0 = [0, len(ATT_B[0])]
ATT_I0 = [0, sum(len(att_items(q)) for q in ATT_B[0])]


def items_before(layer, q):
    return ATT_I0[layer] + sum(len(att_items(x)) for x in ATT_B[layer][:q])


def span(layer, n):
    kind = CHUNKS[n][0]
    return (N_META, SEQ // 2) if layer == DEPTH - 1 and kind in ("q", "gate", "out") else (0, T // 2)


def blk(b):
    return slice(0, N_META) if b == 0 else slice(N_META + P * (b - 1), N_META + P * b)


LEVELS = [1, 2, 4, 8, 16, 32, 64]
TAIL = T - 4 * P


def level_cols(s):
    return T if 2 * s <= TAIL else 4 * P


def build(nc, xT, w_in, w_out, prm, pool_w, c_rope, c_f32, c_mask, outT, h1T):
    ctx = ExitStack()
    with ctx:
        top = [0]
        base = -(-nc.sbuf_base // 64) * 64

        def place(name, shape, dt, at=None):
            size = int(np.prod(shape[1:])) * (1 if dt == U8 else 4)
            size = -(-size // 32) * 32
            if at is None:
                at = base + top[0]
                top[0] += size
                assert at + size <= nc.sbuf_usable_end, (name, at + size, nc.sbuf_usable_end)
            return nc.alloc_sbuf_tensor_at(name, shape, dt, offset=at), at + size

        U = T * 4
        xh, _ = place("x_hi", [P, KC, T], F32R)
        xl, _ = place("x_lo", [P, KC, T], F32R)
        mh_at = base + top[0]
        mh, _ = place("mixed_hi", [P, KC, T], F32R)
        ml_at = base + top[0]
        ml, _ = place("mixed_lo", [P, KC, T], F32R)
        wst, _ = place("w_stage", [P, 2, KC, P], F32)
        wh, _ = place("w_hi", [P, 2, KC, P], F32R)
        wl, _ = place("w_lo", [P, 2, KC, P], F32R)
        rstd, _ = place("rstd", [P, T], F32)
        prm_sb, _ = place("prm_sb", [P, DEPTH, NPRM], F32)
        pw_sb, _ = place("pool_w_sb", [P, DEPTH, NG, P], F32)
        cst, _ = place("cst", [P, 3 * P + 272 + NG * PAD], F32)
        lmask, _ = place("level_mask", [P, len(LEVELS), 4, 64], U8)
        lmask_f, _ = place("level_mask_f32", [P, len(LEVELS), 64], F32, ml_at)
        coef, _ = place("hgrn_coef", [P, DEPTH, 4, HA], F32)
        lbt, _ = place("lb_tmp", [P, 8, HA], F32)
        stat, _ = place("att_stat", [P, 5, 4, 4], F32)
        z, _ = place("z", [P, 2, PAD + T], F32)
        ta, _ = place("ta", [P, PAD + T], F32)
        tb, _ = place("tb", [P, PAD + T], F32)
        th_at = base + top[0]
        th, _ = place("h_tanh", [P, T], F32)
        vt_at = base + top[0]
        vt, _ = place("h_vt", [P, T], F32)
        vh, _ = place("h_v", [P, 5, P], F32)
        res = [place("res0", [P, T], F32, th_at)[0], place("res1", [P, T], F32, vt_at)[0]]

        y, _ = place("y", [P, KC, T], F32, ml_at)
        pts, a1 = place("a_pt", [P, 4, 2, P], F32, ml_at)
        pmt, a1 = place("a_pmt", [P, P], F32, a1)
        pmc, a1 = place("a_pmeta", [P, 2, 4, N_META], F32, a1)
        on, a1 = place("a_on", [P, 4, 2, DH], F32, a1)
        assert a1 <= ml_at + 4 * U
        kt, a2 = place("a_kt", [P, T], F32, mh_at + 4 * U)
        vb, a2 = place("a_v", [P, NBLK + 1, P], F32, a2)
        vm, a2 = place("a_vmeta", [P, 2, 4, DH], F32, a2)
        pr, a2 = place("a_p", [P, 2, 4, 272], F32, a2)
        assert a2 <= mh_at + 12 * U
        rope, a3 = place("rope", [P, 2, T], F32, mh_at)
        hf, a3 = place("h_f", [P, T], F32, mh_at)
        hk, a3 = place("h_k", [P, T], F32, a3)
        hq, a3 = place("h_q", [P, T], F32, a3)
        hp, a3 = place("h_qp", [P, T], F32, a3)
        tt, a3 = place("h_tot", [P, T], F32, a3)
        am, a3 = place("h_att", [P, 4, P], F32, a3)
        amt, a3 = place("h_att_tail", [P, TAIL], F32, a3)
        kn, a3 = place("h_kn", [P, 4, P], F32, a3)
        st, a3 = place("h_state", [P, 4, P], F32, a3)
        assert a3 <= mh_at + 8 * U
        xin, _ = place("x_in", [P, KC, T], F32, mh_at)

        eye, ones, bones = cst[:, 0:P], cst[:, P:2 * P], cst[:, 2 * P:3 * P]
        amask = cst[:, 3 * P:3 * P + 272]
        recips = cst[:, 3 * P + 272:3 * P + 272 + NG * PAD].rearrange("p (g t) -> p g t", g=NG)
        st_mx, st_neg, st_den, st_es, st_rd = (stat[:, i] for i in range(5))

        G = ctx.enter_context(nc.psum_tensor("ps_gemm", [P, 2, 2, 512], F32))
        M = ctx.enter_context(nc.psum_tensor("ps_mix", [P, 4, 512], F32))

        def sem(name):
            return ctx.enter_context(nc.semaphore(name))

        s_prm, s_x, s_rope = sem("prm_in"), sem("x_in_s"), sem("rope_in")
        s_w = [sem("w_in0"), sem("w_in1")]
        s_whi, s_wlo, s_gemm, s_z = sem("w_hi_done"), sem("w_lo_done"), sem("gemm_done"), sem("z_done")
        s_mini, s_minie = sem("mini_done"), sem("mini_evac")
        s_sq, s_swap, s_rc, s_rt, s_ropeo = (sem("square_done"), sem("swap_done"), sem("recip_done"),
                                             sem("rsqrt_done"), sem("rope_done"))
        s_th, s_thf, s_prod, s_mhi, s_mlo = (sem("tanh_done"), sem("tanh_f_done"), sem("prod_done"),
                                             sem("mixed_hi_done"), sem("mixed_lo_done"))
        s_pool = sem("pooled_done")
        s_avt, s_avb, s_avz, s_avm = sem("a_v_t"), sem("a_v_sb"), sem("a_vmeta_zero"), sem("a_vmeta_in")
        s_asc, s_amx, s_aneg, s_aex, s_aes = (sem("a_scores"), sem("a_masked"), sem("a_negmax"),
                                              sem("a_exp"), sem("a_expsink"))
        s_apt, s_ape, s_apv, s_aoe, s_aot, s_aod, s_apm = (sem("a_pt_ps"), sem("a_pt_sb"), sem("a_pv"),
                                                    sem("a_o_norm"), sem("a_o_t"), sem("a_o_done"), sem("a_pmeta_c"))
        s_hq, s_hk, s_hvt, s_hve = sem("h_q_done"), sem("h_k_done"), sem("h_vt_ps"), sem("h_v_sb")
        s_hl, s_hu, s_hkt, s_hke = sem("h_level"), sem("h_update"), sem("h_kt_ps"), sem("h_kt_sb")
        s_hinc, s_hs, s_ho, s_hoe, s_hsq, s_hy = (sem("h_inc"), sem("h_states"), sem("h_o_ps"),
                                                  sem("h_o_sb"), sem("h_o_sq"), sem("h_y_done"))
        s_xhi, s_xsq, s_xlo, s_ss = sem("x_hi_done"), sem("x_sq_done"), sem("x_lo_done"), sem("x_ss_done")
        s_res = [sem("res_in0"), sem("res_in1")]
        s_sto = [sem("store0"), sem("store1")]
        s_lb = sem("lb_step")
        s_v, s_a = sem("vector_link"), sem("scalar_link")

        def halves(ap, c0, w):
            return ap[:, c0:c0 + 2 * w].rearrange("p (a t) -> p a t", a=2)

        def zs(par):
            return z[:, par, PAD:PAD + T]

        ta_, tb_ = ta[:, PAD:PAD + T], tb[:, PAD:PAD + T]

        def mini_no(layer, n):
            return layer * len(MINI_SLOTS) + MINI_SLOTS.index(n)

        def norm_no(layer, n):
            return layer * len(NORM_SLOTS) + NORM_SLOTS.index(n)

        def tanh_no(layer, n):
            return layer * len(TANH_CHUNKS) + TANH_CHUNKS.index(n)

        def att_at(layer, n, tick, lag):
            tau = (n - ATT_SLOT) * TICKS + tick - ATT_TICK - lag
            return (tau // 4, tau % 4) if 0 <= tau < 4 * len(ATT_B[layer]) else None

        def store(sp, layer, n):
            c = n - N_IN
            N = NC * layer + n
            sp.wait_ge(s_z, N + 1)
            if layer < DEPTH - 1:
                sp.dma_start(h1T[c], zs(N % 2)).then_inc(s_sto[N % 2], 16)
            else:
                sp.dma_start(outT[c], z[:, N % 2, PAD + N_META:PAD + T]).then_inc(s_sto[N % 2], 16)

        def att_pt_out(act, layer, q, i):
            Q = ATT_Q0[layer] + q
            b = ATT_B[layer][q][0]
            nq = N_META if b == 0 else P
            items = att_items(ATT_B[layer][q])
            for x in (i, 4) if i == 3 else (i,):
                if x not in items:
                    continue
                no = items_before(layer, q) + items.index(x)
                act.wait_ge(s_apt, no + 1)
                if Q and x == items[0]:
                    act.wait_ge(s_apv, Q)
                reg = M[:, 2, 0:256]
                if x == 4:
                    act.activation(pmt[0:64, 0:nq], reg[0:64, 0:nq], ACT.Copy).then_inc(s_ape, 1)
                else:
                    first = 0 if b >= 2 else 1
                    act.activation(pts[:, x, first:2], reg[:, first * P:].rearrange("p (s q) -> p s q", q=P),
                                   ACT.Copy).then_inc(s_ape, 1)

        def kind_slot(n):
            return ("hgrn", (n - 21) % 3) if 21 <= n < 21 + 3 * HA else ("", 0)

        block = ctx.enter_context(nc.Block())

        @block.sync
        def _(sp):
            def load_w(N):
                if N >= 2:
                    sp.wait_ge(s_wlo, 4 * (N - 1))
                layer, n = divmod(N, NC)
                src = w_in[layer, n] if n < N_IN else w_out[layer, n - N_IN]
                sp.dma_start(wst[:, N % 2].rearrange("p k c -> p (k c)"), src).then_inc(s_w[N % 2], 16)

            sp.dma_start(xin[:, 0:4], xT[:, 0:4]).then_inc(s_x, 16)
            load_w(0)
            for q in range(1, 4):
                sp.dma_start(xin[:, 4 * q:4 * q + 4], xT[:, 4 * q:4 * q + 4]).then_inc(s_x, 16)
            sp.dma_start(prm_sb[:], prm).then_inc(s_prm, 16)
            sp.dma_start(pw_sb[:].rearrange("p l g c -> p l (g c)"), pool_w).then_inc(s_prm, 16)
            sp.dma_start(cst[:], c_f32).then_inc(s_prm, 16)
            sp.dma_start(lmask_f[:].rearrange("p l i -> p (l i)"), c_mask).then_inc(s_prm, 16)
            load_w(1)
            for N in range(NTOT):
                layer, n = divmod(N, NC)
                if N + 2 < NTOT:
                    load_w(N + 2)
                if n == 0:
                    sp.wait_ge(s_xlo, 16)
                    sp.wait_ge(s_xsq, 16)
                    if layer:
                        sp.wait_ge(s_gemm, NC * layer)
                    sp.dma_start(rope[:], c_rope).then_inc(s_rope, 16)
                if n - 1 in ROPE_CHUNKS:
                    R = NROPE * layer + ROPE_CHUNKS.index(n - 1)
                    sp.wait_ge(s_z, N)
                    if R:
                        sp.wait_ge(s_ropeo, R)
                    for quarter in range(4):
                        a, b = 32 * quarter, 32 * (quarter ^ 1)
                        sp.dma_start(tb[a:a + 32, PAD:PAD + T], z[b:b + 32, (N - 1) % 2, PAD:PAD + T])\
                          .then_inc(s_swap, 16)
                if n == 2:
                    sp.wait_ge(s_avb, 2 * layer + 2)
                    sp.wait_ge(s_avz, layer + 1)
                    for i in range(4):
                        sp.dma_start(vm[16 * i:16 * i + 16, :, i, :],
                                     vb[0:N_META, 0, :].rearrange("p (v d) -> p v d", v=2)).then_inc(s_avm, 16)
                if n >= N_IN - 1:
                    c = n - (N_IN - 1)
                    if c < KC:
                        if c < 2:
                            sp.wait_ge(s_hy, 4 * (layer + 1))
                        else:
                            sp.wait_ge(s_z, NC * layer + N_IN + c - 1)
                        if layer and c == 0:
                            for par in range(2):
                                sp.wait_ge(s_sto[par], 16 * (KC // 2))
                        src = xT[:, c] if layer == 0 else h1T[c]
                        sp.dma_start(res[c % 2][:], src).then_inc(s_res[c % 2], 16)
                if n > N_IN:
                    store(sp, layer, n - 1)
                if n == 0 and layer:
                    store(sp, layer - 1, NC - 1)
            store(sp, DEPTH - 1, NC - 1)
            for par in range(2):
                sp.wait_ge(s_sto[par], 16 * (KC // 2) * DEPTH)

        @block.gpsimd
        def _(pool):
            for layer in range(DEPTH):
                if layer:
                    pool.wait_ge(s_gemm, NC * layer)
                else:
                    pool.wait_ge(s_xlo, 16)
                    pool.wait_ge(s_xsq, 16)
                pool.memset(vm[:], 0.0).then_inc(s_avz, 1)

        @block.scalar
        def _(act):
            def w_high(N, q):
                if q == 0:
                    act.wait_ge(s_w[N % 2], 16 * (N // 2 + 1))
                    if N >= 2:
                        act.wait_ge(s_gemm, N - 1)
                act.activation(wh[:, N % 2, 4 * q:4 * q + 4], wst[:, N % 2, 4 * q:4 * q + 4], ACT.Copy)\
                   .then_inc(s_whi, 1)

            def x_split(layer, k, src):
                g = prm_sb[:, layer, C_NORM + k:C_NORM + k + 1]
                act.activation(xh[:, k], src, ACT.Copy, scale=g).then_inc(s_xhi, 1)
                if 16 * layer + k:
                    act.wait_ge(s_ss, 16 * layer + k)
                act.activation(ta_, src, ACT.Square).then_inc(s_xsq, 1)

            act.wait_ge(s_prm, 64)
            for q in range(4):
                w_high(0, q)
            act.wait_ge(s_lb, 1)
            act.activation(lbt[:, 2:4], lbt[:, 0:2], ACT.Exp).then_inc(s_lb, 1)
            for k in range(KC):
                if k % 4 == 0:
                    act.wait_ge(s_x, 64)
                x_split(0, k, xin[:, k])

            for N in range(NTOT):
                layer, n = divmod(N, NC)
                for tick in range(TICKS):
                    if tick == 0 and N:
                        pl, pn = divmod(N - 1, NC)
                        kind, idx = CHUNKS[pn]
                        zz = zs((N - 1) % 2)
                        c0, w = span(pl, pn)
                        cols = slice(c0, c0 + 2 * w)
                        act.wait_ge(s_z, N)
                        if kind in ("k", "q"):
                            R = NROPE * layer + ROPE_CHUNKS.index(pn)
                            if R:
                                act.wait_ge(s_ropeo, R)
                            act.activation(ta_[:, cols], zz[:, cols], ACT.Square).then_inc(s_sq, 1)
                        elif kind in ("gate", "hq"):
                            act.activation(ta_[:, cols], zz[:, cols], ACT.Tanh, scale=0.5).then_inc(s_th, 1)
                        elif kind == "hf":
                            if 4 * pl + idx:
                                act.wait_ge(s_hk, 4 * pl + idx)
                            act.activation(th[:], zz, ACT.Tanh, scale=0.5).then_inc(s_thf, 1)
                        elif kind == "out" and pl < DEPTH - 1:
                            x_split(pl + 1, idx, zz)
                    if tick == 2 and N and CHUNKS[(N - 1) % NC][0] == "gate":
                        pl, pn = divmod(N - 1, NC)
                        gno = len(GATES) * pl + GATES.index(CHUNKS[pn][1])
                        c0, w = span(pl, pn)
                        act.wait_ge(s_prod, gno + 1)
                        m = CHUNKS[pn][1]
                        act.activation(mh[:, m, c0:c0 + 2 * w], zs((N - 1) % 2)[:, c0:c0 + 2 * w], ACT.Copy)\
                           .then_inc(s_mhi, 1)
                    if tick % 4 == 1 and N + 1 < NTOT:
                        w_high(N + 1, tick // 4)
                    if n in NORM_SLOTS and tick == MINI_TICK + 3:
                        kind, idx = MINI[n]
                        no = norm_no(layer, n)
                        act.wait_ge(s_rc, no + 1)
                        if kind == "rms":
                            act.activation(rstd[:], rstd[:], ACT.Sqrt).then_inc(s_rt, 1)
                        else:
                            buf = ta_ if kind == "rope" else tb_
                            c0, w = span(layer, n - 1) if kind == "rope" else (0, T // 2)
                            act.activation(buf[:, c0:c0 + 2 * w], buf[:, c0:c0 + 2 * w], ACT.Sqrt).then_inc(s_rt, 1)
                    if n == 2 and tick == 2:
                        act.wait_ge(s_avt, layer + 1)
                        act.activation(vb[:, 1:NBLK + 1], M[:, 0].rearrange("p (b c) -> p b c", b=NBLK), ACT.Copy)\
                           .then_inc(s_avb, 1)
                        act.activation(vb[0:N_META, 0], M[0:N_META, 1, 0:P], ACT.Copy).then_inc(s_avb, 1)
                    at = att_at(layer, n, tick, 4)
                    if at:
                        q, i = at
                        Q = ATT_Q0[layer] + q
                        b = ATT_B[layer][q][0]
                        nq = N_META if b == 0 else P
                        lo = (256, 128, 0)[min(b, 2)]
                        if i == 0:
                            act.wait_ge(s_aneg, Q + 1)
                            act.activation(st_es[0:nq, Q % 4], st_es[0:nq, Q % 4], ACT.Exp).then_inc(s_aes, 1)
                        act.activation(pr[0:nq, Q % 2, i, lo:272], pr[0:nq, Q % 2, i, lo:272], ACT.Exp,
                                       bias=st_neg[0:nq, Q % 4, i:i + 1],
                                       accum_out=st_den[0:nq, Q % 4, i:i + 1]).then_inc(s_aex, 1)
                    at = att_at(layer, n, tick, 5)
                    if at:
                        att_pt_out(act, layer, *at)
                    if kind_slot(n) == ("hgrn", 0):
                        H = 4 * layer + (n - 21) // 3
                        if tick == 4:
                            act.wait_ge(s_hvt, H + 1)
                            if H:
                                act.wait_ge(s_ho, H)
                            act.activation(vh[:, 0:4], M[:, 3].rearrange("p (b c) -> p b c", b=4), ACT.Copy)\
                               .then_inc(s_hve, 1)
                            act.activation(vh[0:TAIL, 4], M[0:TAIL, 2, 0:P], ACT.Copy).then_inc(s_hve, 1)
                    if kind_slot(n) == ("hgrn", 1):
                        H = 4 * layer + (n - 22) // 3
                        if tick == 2:
                            act.wait_ge(s_hkt, H + 1)
                            act.activation(kn[:], M[:, 0].rearrange("p (b c) -> p b c", b=4), ACT.Copy)\
                               .then_inc(s_hke, 1)
                        if tick == 6:
                            act.wait_ge(s_hoe, H + 1)
                            act.activation(tb_, y[:, H % 4], ACT.Square).then_inc(s_hsq, 1)

        @block.tensor
        def _(pe):
            def mini(N, layer, n):
                kind, idx = MINI[n]
                no = mini_no(layer, n)
                g = G[:, (N + 1) % 2]
                c0, w = (0, T // 2)
                if N:
                    pe.wait_ge(s_z, N)
                if kind == "rms":
                    pe.wait_ge(s_ss, 16 * layer + 16)
                    lhs, rhs = ones, rstd
                elif kind == "rope":
                    c0, w = span(layer, n - 1)
                    pe.wait_ge(s_sq, NROPE * layer + idx + 1)
                    lhs, rhs = bones, ta_
                elif kind == "pool":
                    pe.wait_ge(s_pool, NG * layer + idx + 1)
                    lhs, rhs = pw_sb[:, layer, idx], ta_
                else:
                    pe.wait_ge(s_hsq, 4 * layer + idx + 1)
                    lhs, rhs = ones, tb_
                for half in range(2):
                    ins = pe.matmul(g[:, half, 0:w], lhs, rhs[:, c0 + half * w:c0 + half * w + w],
                                    start=True, stop=True)
                ins.then_inc(s_mini, 1)

            def scores(layer, q, i):
                Q = ATT_Q0[layer] + q
                b, j, kv = ATT_B[layer][q]
                J = 4 * Q + i
                rows = slice(64 * kv, 64 * kv + 64)
                qT = y[rows, 4 + 4 * j + i, blk(b)]
                nq = qT.shape[1]
                if q == 0 and i == 0:
                    pe.wait_ge(s_ropeo, NROPE * (layer + 1))
                    pe.wait_ge(s_avb, 2 * layer + 2)
                if J >= 2:
                    pe.wait_ge(s_amx, J - 1)
                if b >= 1:
                    lo, first = (P, blk(b).start) if b == 1 else (0, blk(b - 1).start)
                    pe.matmul(M[0:nq, J % 2, lo:256], qT, kt[rows, first:blk(b).stop], start=True, stop=True)
                pe.matmul(M[0:nq, J % 2, 256:272], qT, kt[rows, 0:N_META], start=True, stop=True)\
                  .then_inc(s_asc, 1)

            def probs_t(layer, q, i):
                Q = ATT_Q0[layer] + q
                b = ATT_B[layer][q][0]
                nq = N_META if b == 0 else P
                items = att_items(ATT_B[layer][q])
                for x in (i, 4) if i == 3 else (i,):
                    if x not in items:
                        continue
                    no = items_before(layer, q) + items.index(x)
                    if x == 4:
                        pe.wait_ge(s_apm, Q + 1)
                    else:
                        pe.wait_ge(s_aex, 4 * Q + x + 1)
                    if no >= 1:
                        pe.wait_ge(s_ape, no)
                    c = 0
                    if x == 4:
                        ins = pe.transpose(M[0:64, 2, c:c + nq], pmc[0:nq, Q % 2].rearrange("p i k -> p (i k)"),
                                           eye[0:nq, 0:nq])
                    else:
                        for s in range(0 if b >= 2 else 1, 2):
                            ins = pe.transpose(M[:, 2, c + P * s:c + P * s + P],
                                               pr[:, Q % 2, x, P * s:P * s + P], eye)
                    ins.then_inc(s_apt, 1)

            def values(layer, q):
                Q = ATT_Q0[layer] + q
                b, j, kv = ATT_B[layer][q]
                nq = N_META if b == 0 else P
                pe.wait_ge(s_ape, items_before(layer, q + 1))
                if q == 0:
                    pe.wait_ge(s_avm, 64 * (layer + 1))
                if Q >= 1:
                    pe.wait_ge(s_aoe, Q)
                if kv == 0 and Q >= 2:
                    pe.wait_ge(s_aod, Q // 2)
                o = M[0:nq, 3, 256 * kv:256 * kv + 256]
                last = pe.matmul(o, pmt[0:64, 0:nq], vm[0:64, kv].rearrange("p i d -> p (i d)"),
                                 start=True, stop=b == 0)
                if b:
                    for i in range(4):
                        for s in range(0 if b >= 2 else 1, 2):
                            last = pe.matmul(o[:, DH * i:DH * i + DH], pts[:, i, s],
                                             vb[:, b - 1 + s, DH * kv:DH * kv + DH],
                                             start=False, stop=i == 3 and s == 1)
                last.then_inc(s_apv, 1)

            def outputs_t(layer, q):
                Q = ATT_Q0[layer] + q
                b = ATT_B[layer][q][0]
                nq = N_META if b == 0 else P
                pe.wait_ge(s_aoe, Q + 1)
                for i in range(4):
                    ins = pe.transpose(M[:, 3, P * i:P * i + nq], on[0:nq, i].rearrange("p v d -> p (v d)"),
                                       eye[0:nq, 0:nq])
                ins.then_inc(s_aot, 1)

            def hgrn_level(layer, H, l):
                bank = M[:, l % 2]
                pe.wait_ge(s_hk, H + 1)
                if l == 0:
                    if H == 4 * layer:
                        pe.wait_ge(s_amx, 4 * (ATT_Q0[layer] + len(ATT_B[layer])))
                    if H:
                        pe.wait_ge(s_hs, H)
                else:
                    pe.wait_ge(s_hu, 8 * H + l)
                for b in range(4):
                    kcols = slice(P * b, P * b + P)
                    if l == 0:
                        ins = pe.matmul(bank[:, kcols], hk[:, kcols], hq[:, kcols], start=True, stop=True)
                    else:
                        s = LEVELS[l - 1]
                        rhs = hp[:, kcols].rearrange("p (g two s) -> p g two s", two=2, s=s)[:, :, 1]
                        ins = pe.matmul(bank[:, 64 * b:64 * b + 64], hk[:, kcols], rhs, start=True, stop=True)
                kcols = slice(4 * P, T)
                if l == 0:
                    ins = pe.matmul(M[0:TAIL, 1, 0:TAIL], hk[:, kcols], hq[:, kcols], start=True, stop=True)
                elif level_cols(LEVELS[l - 1]) == T:
                    s = LEVELS[l - 1]
                    rhs = hp[:, kcols].rearrange("p (g two s) -> p g two s", two=2, s=s)[:, :, 1]
                    ins = pe.matmul(bank[0:TAIL, 256:256 + TAIL // 2], hk[:, kcols], rhs, start=True, stop=True)
                ins.then_inc(s_hl, 1)

            def hgrn_v_t(H):
                pe.wait_ge(s_z, NC * (H // 4) + 21 + 3 * (H % 4))
                if H % 4:
                    pe.wait_ge(s_hoe, H)
                else:
                    pe.wait_ge(s_aod, (ATT_Q0[H // 4] + len(ATT_B[H // 4])) // 2)
                    pe.wait_ge(s_ape, items_before(H // 4, len(ATT_B[H // 4])))
                for b in range(4):
                    pe.transpose(M[:, 3, P * b:P * b + P], vt[:, P * b:P * b + P], eye)
                pe.transpose(M[0:TAIL, 2, 0:P], vt[:, 4 * P:T], eye).then_inc(s_hvt, 1)

            def hgrn_k_t(H):
                pe.wait_ge(s_hu, 8 * H + 8)
                for b in range(4):
                    ins = pe.transpose(M[:, 0, P * b:P * b + P], hk[:, P * b:P * b + P], eye)
                ins.then_inc(s_hkt, 1)

            def hgrn_increments(H):
                pe.wait_ge(s_hke, H + 1)
                pe.wait_ge(s_hve, 2 * H + 2)
                for b in range(4):
                    ins = pe.matmul(M[:, 1, P * b:P * b + P], kn[:, b], vh[:, b], start=True, stop=True)
                ins.then_inc(s_hinc, 1)

            def hgrn_out(H):
                pe.wait_ge(s_hs, H + 1)
                for b in range(5):
                    cols = slice(P * b, min(P * b + P, T))
                    o = M[:, 3, cols] if b < 4 else M[:, 2, 0:TAIL]
                    lhs = vh[:, b] if b < 4 else vh[0:TAIL, 4]
                    rhs = am[:, b] if b < 4 else amt[0:TAIL]
                    ins = pe.matmul(o, lhs, rhs, start=True, stop=b == 0)
                    if b:
                        ins = pe.matmul(o, st[:, b - 1], hp[:, cols], start=False, stop=True)
                ins.then_inc(s_ho, 1)

            pe.wait_ge(s_prm, 64)
            for N in range(NTOT):
                layer, n = divmod(N, NC)
                g = G[:, N % 2]
                c0, w = span(layer, n)
                if N >= 2:
                    pe.wait_ge(s_z, N - 1)
                pl, pn = divmod(N - 1, NC)
                if N and pn in MINI:
                    pe.wait_ge(s_minie, mini_no(pl, pn) + 1)
                for tick in range(TICKS):
                    k = tick if n < N_IN else GATES[tick]
                    if tick % 4 == 0:
                        pe.wait_ge(s_wlo, 4 * N + tick // 4 + 1)
                    if n == 0:
                        pe.wait_ge(s_xlo, 16 * layer + tick + 1)
                    if n == N_IN:
                        pe.wait_ge(s_mlo, len(GATES) * layer + tick + 1)
                    hi, lo = (xh, xl) if n < N_IN else (mh, ml)
                    passes = ((wh, hi), (wh, lo), (wl, hi))
                    for i, (ws, xs) in enumerate(passes):
                        for half in range(2):
                            ins = pe.matmul(g[:, half, 0:w], ws[:, N % 2, tick],
                                            xs[:, k, c0 + half * w:c0 + half * w + w],
                                            start=tick == 0 and i == 0, stop=tick == TICKS - 1 and i == 2)
                    if tick == TICKS - 1:
                        ins.then_inc(s_gemm, 1)
                    if n in MINI and tick == MINI_TICK:
                        mini(N, layer, n)
                    if n == 2 and tick == 1:
                        pe.wait_ge(s_z, N)
                        if layer:
                            pe.wait_ge(s_hs, 4 * layer)
                        vz = zs((N - 1) % 2)
                        for b in range(NBLK):
                            pe.transpose(M[:, 0, P * b:P * b + P], vz[:, blk(b + 1)], eye)
                        pe.transpose(M[0:N_META, 1, 0:P], vz[:, 0:N_META], eye).then_inc(s_avt, 1)
                    at = att_at(layer, n, tick, 0)
                    if at:
                        scores(layer, *at)
                    at = att_at(layer, n, tick, 9)
                    if at and at[1] == 0:
                        values(layer, at[0])
                    at = att_at(layer, n, tick, 5)
                    if at:
                        probs_t(layer, *at)
                    at = att_at(layer, n, tick, 10)
                    if at and at[1] == 0 and ATT_B[layer][at[0]][2] == 1:
                        outputs_t(layer, at[0])
                    if kind_slot(n) == ("hgrn", 0):
                        H = 4 * layer + (n - 21) // 3
                        if tick == 1:
                            hgrn_v_t(H)
                        if tick % 2 == 1:
                            hgrn_level(layer, H, tick // 2)
                    if kind_slot(n) == ("hgrn", 1):
                        H = 4 * layer + (n - 22) // 3
                        if tick == 1:
                            hgrn_k_t(H)
                        if tick == 3:
                            hgrn_increments(H)
                        if tick == 5:
                            hgrn_out(H)

        @block.vector
        def _(dve):
            links = [0]

            def link(ins):
                links[0] += 1
                ins.then_inc(s_v, 1)
                dve.wait_ge(s_v, links[0])

            counts = {}

            def signal(ins, s):
                counts[s.name] = counts[s.name] + 1 if s.name in counts else 1
                ins.then_inc(s, 1)
                dve.wait_ge(s, counts[s.name])

            def w_low(N, q):
                dve.wait_ge(s_whi, 4 * N + q + 1)
                part = (slice(None), N % 2, slice(4 * q, 4 * q + 4))
                dve.tensor_tensor(wl[part], wst[part], wh[part].bitcast(F32), ALU.subtract).then_inc(s_wlo, 1)

            def x_low(layer, k, src):
                g = prm_sb[:, layer, C_NORM + k:C_NORM + k + 1]
                dve.wait_ge(s_xhi, 16 * layer + k + 1)
                signal(dve.scalar_tensor_tensor(xl[:, k], src, g, xh[:, k].bitcast(F32), ALU.mult, ALU.subtract), s_xlo)
                dve.wait_ge(s_xsq, 16 * layer + k + 1)
                if k == 0:
                    signal(dve.tensor_copy(rstd[:], ta_), s_ss)
                else:
                    dve.wait_ge(s_ss, 16 * layer + k)
                    signal(dve.tensor_tensor(rstd[:], rstd[:], ta_, ALU.add), s_ss)

            link(dve.memset(z[:, :, 0:PAD], 0.0))
            link(dve.memset(ta[:, 0:PAD], 0.0))
            link(dve.memset(tb[:, 0:PAD], 0.0))
            dve.wait_ge(s_prm, 64)
            for b in range(4):
                link(dve.tensor_copy(lmask[:, :, b], lmask_f[:]))
            l0, l1 = prm_sb[:, 0, C_LB:C_LB + HA], prm_sb[:, 0, C_LB + HA:C_LB + 2 * HA]
            link(dve.tensor_tensor(lbt[:, 4], l0, l1, ALU.max))
            link(dve.tensor_tensor(lbt[:, 0], l0, lbt[:, 4], ALU.subtract))
            dve.tensor_tensor(lbt[:, 1], l1, lbt[:, 4], ALU.subtract).then_inc(s_lb, 1)
            for q in range(4):
                w_low(0, q)
            dve.wait_ge(s_lb, 2)
            link(dve.tensor_tensor(lbt[:, 4], lbt[:, 2], lbt[:, 3], ALU.add))
            link(dve.reciprocal(lbt[:, 5], lbt[:, 4]))
            link(dve.tensor_tensor(lbt[:, 2], lbt[:, 2], lbt[:, 5], ALU.mult))
            link(dve.tensor_tensor(lbt[:, 3], lbt[:, 3], lbt[:, 5], ALU.mult))
            link(dve.tensor_tensor(lbt[:, 6], lbt[:, 2], lbt[:, 2], ALU.subtract))
            link(dve.tensor_tensor(lbt[:, 7], lbt[:, 2], lbt[:, 3], ALU.add))
            link(dve.tensor_tensor(lbt[:, 7], lbt[:, 7], lbt[:, 2], ALU.subtract))
            for layer in range(DEPTH):
                lb, (a, b, na, ha) = lbt[:, 6 + layer], (coef[:, layer, i] for i in range(4))
                link(dve.tensor_scalar(a, lb, -0.5, 0.5, ALU.mult, ALU.add))
                link(dve.tensor_tensor(b, lb, a, ALU.add))
                link(dve.tensor_scalar(na, a, -0.5, None, ALU.mult))
                link(dve.tensor_scalar(ha, a, 0.5, None, ALU.mult))
            for k in range(KC):
                x_low(0, k, xin[:, k])

            def take_out(N):
                layer, n = divmod(N, NC)
                kind, idx = CHUNKS[n]
                c0, w = span(layer, n)
                zz = zs(N % 2)
                src = G[:, N % 2, :, 0:w]
                dve.wait_ge(s_gemm, N + 1)
                if kind == "out":
                    dve.wait_ge(s_res[idx % 2], 16 * (KC // 2 * layer + idx // 2 + 1))
                    if KC * layer + idx >= 2:
                        dve.wait_ge(s_sto[N % 2], 16 * ((KC * layer + idx) // 2))
                    if layer == DEPTH - 1 and idx == 0:
                        pass
                    signal(dve.tensor_tensor(halves(zz, c0, w), src, halves(res[idx % 2], c0, w), ALU.add), s_z)
                    return
                if layer and n < 2:
                    dve.wait_ge(s_sto[N % 2], 16 * (KC // 2) * layer)
                if n == 0:
                    dve.wait_ge(s_rt, norm_no(layer, 0) + 1)
                dst = zz
                if kind == "hi":
                    dst = vt
                    if 4 * layer + idx:
                        dve.wait_ge(s_hvt, 4 * layer + idx)
                signal(dve.tensor_tensor(halves(dst, c0, w), src, halves(rstd, c0, w), ALU.mult), s_z)

            def rope_first(N):
                layer, n = divmod(N, NC)
                kind = CHUNKS[n][0]
                R = NROPE * layer + ROPE_CHUNKS.index(n)
                c0, w = span(layer, n)
                c = slice(c0, c0 + 2 * w)
                gcol = C_KG if kind == "k" else C_QG
                g, gs = (prm_sb[:, layer, gcol + i:gcol + i + 1] for i in range(2))
                zz = zs(N % 2)
                dve.wait_ge(s_rope, 16 * (layer + 1))
                dve.wait_ge(s_sq, R + 1)
                dve.wait_ge(s_swap, 64 * (R + 1))
                link(dve.scalar_tensor_tensor(tb_[:, c], tb_[:, c], gs, rope[:, 1, c], ALU.mult, ALU.mult))
                link(dve.scalar_tensor_tensor(zz[:, c], zz[:, c], g, rope[:, 0, c], ALU.mult, ALU.mult))
                link(dve.tensor_tensor(zz[:, c], zz[:, c], tb_[:, c], ALU.add))

            def rope_last(N):
                layer, n = divmod(N, NC)
                kind, idx = CHUNKS[n]
                c0, w = span(layer, n)
                c = slice(c0, c0 + 2 * w)
                dve.wait_ge(s_rt, norm_no(layer, n + 1) + 1)
                dst = kt[:, c] if kind == "k" else y[:, 4 + idx, c]
                R = NROPE * layer + ROPE_CHUNKS.index(n)
                signal(dve.tensor_tensor(dst, zs(N % 2)[:, c], ta_[:, c], ALU.mult), s_ropeo)

            def mini_out(N):
                layer, n = divmod(N, NC)
                kind, idx = MINI[n]
                no = mini_no(layer, n)
                dve.wait_ge(s_mini, no + 1)
                c0, w = span(layer, n - 1) if kind == "rope" else (0, T // 2)
                src = G[:, (N + 1) % 2, :, 0:w]
                if kind == "pool":
                    signal(dve.tensor_scalar(halves(y[:, 12 + idx], 0, w), src, prm_sb[:, layer, C_PS + idx:C_PS + idx + 1],
                                      None, ALU.mult), s_minie)
                    return
                dst, size = {"rms": (rstd, D_MODEL), "rope": (ta_, DH), "hnorm": (tb_, P)}[kind]
                signal(dve.tensor_scalar(halves(dst, c0, w), src, 1.0 / size, EPS, ALU.mult, ALU.add), s_minie)
                dve.wait_ge(s_minie, no + 1)
                signal(dve.reciprocal(dst[:, c0:c0 + 2 * w], dst[:, c0:c0 + 2 * w]), s_rc)

            def pooling(N):
                layer, n = divmod(N, NC)
                g = CHUNKS[n][1]
                u = z[:, N % 2]
                cur, d = u, 1
                if g == 0:
                    dve.wait_ge(s_ropeo, NROPE * (layer + 1))
                else:
                    dve.wait_ge(s_minie, mini_no(layer, 11 + g - 1) + 1)
                bufs = [ta[:], tb[:]]
                step = 0 if g % 2 == 1 else 1
                while d < WINDOWS[g]:
                    nxt = bufs[step % 2]
                    link(dve.tensor_tensor(nxt[:, PAD:], cur[:, PAD:], cur[:, PAD - d:PAD + T - d], ALU.add))
                    cur, d, step = nxt, 2 * d, step + 1
                link(dve.tensor_tensor(ta[:, PAD:2 * PAD], cur[:, PAD:2 * PAD], recips[:, g], ALU.mult))
                link(dve.tensor_tensor(ta[:, PAD:2 * PAD], ta[:, PAD:2 * PAD], u[:, PAD:2 * PAD], ALU.subtract))
                signal(dve.scalar_tensor_tensor(ta[:, 2 * PAD:], cur[:, 2 * PAD:], 1.0 / WINDOWS[g], u[:, 2 * PAD:],
                                         ALU.mult, ALU.subtract), s_pool)

            def gate_product(N):
                layer, n = divmod(N, NC)
                m = CHUNKS[n][1]
                c0, w = span(layer, n)
                c = slice(c0, c0 + 2 * w)
                zz = zs(N % 2)
                dve.wait_ge(s_th, tanh_no(layer, n) + 1)
                link(dve.scalar_tensor_tensor(zz[:, c], ta_[:, c], 1.0, zz[:, c], ALU.add, ALU.mult))
                if m == 8:
                    dve.wait_ge(s_aod, (ATT_Q0[layer] + len(ATT_B[layer])) // 2)
                if m < HA:
                    dve.wait_ge(s_hy, 4 * layer + m + 1)
                signal(dve.scalar_tensor_tensor(zz[:, c], zz[:, c], 0.5, y[:, m, c], ALU.mult, ALU.mult), s_prod)

            def gate_low(N):
                layer, n = divmod(N, NC)
                m = CHUNKS[n][1]
                c0, w = span(layer, n)
                c = slice(c0, c0 + 2 * w)
                dve.wait_ge(s_mhi, len(GATES) * layer + GATES.index(m) + 1)
                signal(dve.tensor_tensor(ml[:, m, c], zs(N % 2)[:, c], mh[:, m, c].bitcast(F32), ALU.subtract), s_mlo)

            def att_mask_max(layer, q, i):
                Q = ATT_Q0[layer] + q
                b, j, kv = ATT_B[layer][q]
                J = 4 * Q + i
                nq = N_META if b == 0 else P
                lo = (256, 128, 0)[min(b, 2)]
                head = GRP * kv + 4 * j + i
                sink = prm_sb[0:nq, layer, C_SINK + head:C_SINK + head + 1]
                mask = amask[0:nq, P:P + N_META] if b == 0 else amask[:, lo:272]
                dve.wait_ge(s_asc, J + 1)
                if Q >= 2 and i == 0:
                    lq = (layer, q - 2) if q >= 2 else (layer - 1, len(ATT_B[layer - 1]) + q - 2)
                    dve.wait_ge(s_apt, items_before(lq[0], lq[1] + 1))
                signal(dve.tensor_tensor_reduce(pr[0:nq, Q % 2, i, lo:272], M[0:nq, J % 2, lo:272], mask, DH ** -0.5,
                                         sink, ALU.add, ALU.max, st_mx[0:nq, Q % 4, i:i + 1]), s_amx)
                if i == 3:
                    dve.wait_ge(s_amx, J + 1)
                    link(dve.tensor_scalar(st_neg[0:nq, Q % 4], st_mx[0:nq, Q % 4], -1.0, None, ALU.mult))
                    sinks = prm_sb[0:nq, layer, C_SINK + head - 3:C_SINK + head + 1]
                    signal(dve.tensor_tensor(st_es[0:nq, Q % 4], sinks, st_mx[0:nq, Q % 4], ALU.subtract), s_aneg)

            def att_meta(layer, q):
                Q = ATT_Q0[layer] + q
                nq = N_META if ATT_B[layer][q][0] == 0 else P
                dve.wait_ge(s_aex, 4 * Q + 4)
                if Q >= 2:
                    lq = (layer, q - 2) if q >= 2 else (layer - 1, len(ATT_B[layer - 1]) + q - 2)
                    dve.wait_ge(s_apt, items_before(lq[0], lq[1] + 1))
                signal(dve.tensor_copy(pmc[0:nq, Q % 2], pr[0:nq, Q % 2, :, 256:272]), s_apm)

            def att_normalise(layer, q):
                Q = ATT_Q0[layer] + q
                b, j, kv = ATT_B[layer][q]
                nq = N_META if b == 0 else P
                dve.wait_ge(s_aex, 4 * Q + 4)
                link(dve.tensor_tensor(st_rd[0:nq, Q % 4], st_den[0:nq, Q % 4], st_es[0:nq, Q % 4], ALU.add))
                link(dve.reciprocal(st_rd[0:nq, Q % 4], st_rd[0:nq, Q % 4]))
                dve.wait_ge(s_apv, Q + 1)
                rd = st_rd[0:nq, Q % 4].unsqueeze(2).broadcast_to([nq, 4, DH])
                signal(dve.tensor_tensor(on[0:nq, :, kv], M[0:nq, 3, 256 * kv:256 * kv + 256]
                                  .rearrange("p (i d) -> p i d", i=4), rd, ALU.mult), s_aoe)

            def att_out(layer, q):
                Q = ATT_Q0[layer] + q
                b, j, kv = ATT_B[layer][q]
                nq = N_META if b == 0 else P
                dve.wait_ge(s_aot, Q // 2 + 1)
                signal(dve.tensor_copy(y[:, 4 + 4 * j:8 + 4 * j, blk(b)],
                                M[:, 3].rearrange("p (i q) -> p i q", i=4)[:, :, 0:nq]), s_aod)

            def hgrn_prepare(layer, h):
                H = 4 * layer + h
                a, b, na, ha = (coef[:, layer, i, h:h + 1] for i in range(4))
                dve.wait_ge(s_thf, H + 1)
                if H:
                    dve.wait_ge(s_ho, H)
                link(dve.tensor_scalar(hf[:], th[:], a, b, ALU.mult, ALU.add))
                link(dve.tensor_scalar(hf[:], hf[:], LOG_FLOOR, None, ALU.max))
                link(dve.tensor_scalar(hk[:], th[:], na, ha, ALU.mult, ALU.add))
                signal(dve.tensor_tensor(hp[:], hq[:], hf[:], ALU.mult), s_hk)
                dve.wait_ge(s_hk, H + 1)

            def hgrn_level_out(layer, H, l):
                dve.wait_ge(s_hl, 8 * H + l + 1)
                bank = M[:, l % 2]
                if l == 0:
                    e4 = eye.unsqueeze(1).broadcast_to([P, 4, P])
                    dve.tensor_tensor(am[:], bank.rearrange("p (b i) -> p b i", b=4), e4, ALU.mult)\
                       .then_inc(s_v, 1)
                    signal(dve.tensor_tensor(amt[0:TAIL], M[0:TAIL, 1, 0:TAIL], eye[0:TAIL, 0:TAIL], ALU.mult), s_hu)
                    links[0] += 1
                    dve.wait_ge(s_v, links[0])
                    dve.wait_ge(s_hu, 8 * H + 1)
                    return
                s = LEVELS[l - 1]
                cols = level_cols(s)
                ng = cols // (2 * s)
                amv = am[:].rearrange("p b i -> p (b i)").rearrange("p (g two s) -> p g two s", two=2, s=s)
                link(dve.copy_predicated(amv[:, :, 1], lmask[:, l - 1].rearrange("p b i -> p (b i)").rearrange("p (g s) -> p g s", s=s),
                                         bank[:, 0:256].rearrange("p (g s) -> p g s", s=s)))
                if cols == T:
                    atv = amt[0:TAIL].rearrange("p (g two s) -> p g two s", two=2, s=s)
                    link(dve.copy_predicated(atv[:, :, 1],
                                             lmask[0:TAIL, l - 1, 0, 0:TAIL // 2].rearrange("p (g s) -> p g s", s=s),
                                             bank[0:TAIL, 256:256 + TAIL // 2].rearrange("p (g s) -> p g s", s=s)))
                off = {1: None, 2: 0, 4: 264, 8: 396, 16: 462, 32: 495, 64: 511, 128: 519}
                cur = hf[:] if s == 1 else tt[:, off[s]:off[s] + 2 * ng]
                pair = cur[:, 0:2 * ng].rearrange("p (g two) -> p g two", two=2)
                qv = hp[:, 0:cols].rearrange("p (g two s) -> p g two s", two=2, s=s)
                kv = hk[:, 0:cols].rearrange("p (g two s) -> p g two s", two=2, s=s)
                link(dve.tensor_tensor(tt[:, off[2 * s]:off[2 * s] + ng], pair[:, :, 0], pair[:, :, 1], ALU.mult))
                link(dve.tensor_tensor(qv[:, :, 1], qv[:, :, 1],
                                       pair[:, :, 0].unsqueeze(2).broadcast_to([P, ng, s]), ALU.mult))
                signal(dve.tensor_tensor(kv[:, :, 0], kv[:, :, 0],
                                  pair[:, :, 1].unsqueeze(2).broadcast_to([P, ng, s]), ALU.mult), s_hu)
                dve.wait_ge(s_hu, 8 * H + l + 1)

            def hgrn_states(H):
                dve.wait_ge(s_hinc, H + 1)
                link(dve.tensor_copy(st[:, 0], M[:, 1, 0:P]))
                for b in range(1, 4):
                    ins = dve.scalar_tensor_tensor(st[:, b], st[:, b - 1], tt[:, 519 + b:520 + b],
                                                   M[:, 1, P * b:P * b + P], ALU.mult, ALU.add)
                    if b < 3:
                        link(ins)
                signal(ins, s_hs)

            def hgrn_take_out(H):
                dve.wait_ge(s_ho, H + 1)
                link(dve.tensor_copy(y[:, H % 4, 0:4 * P], M[:, 3]))
                signal(dve.tensor_copy(y[:, H % 4, 4 * P:T], M[:, 2, 0:TAIL]), s_hoe)

            def hgrn_norm(layer, H):
                dve.wait_ge(s_rt, norm_no(layer, 22 + 3 * (H % 4)) + 1)
                signal(dve.scalar_tensor_tensor(y[:, H % 4], y[:, H % 4], prm_sb[:, layer, C_HG:C_HG + 1], tb_,
                                         ALU.mult, ALU.mult), s_hy)

            for N in range(NTOT):
                layer, n = divmod(N, NC)
                pkind, pidx = CHUNKS[(N - 1) % NC] if N else ("", 0)
                for tick in range(TICKS):
                    if tick == 0 and N:
                        take_out(N - 1)
                    if tick == 1 and N >= 2 and CHUNKS[(N - 2) % NC][0] in ("k", "q"):
                        rope_last(N - 2)
                    if tick == 1:
                        if pkind == "gate":
                            gate_product(N - 1)
                        if pkind == "hq":
                            pl, pn = divmod(N - 1, NC)
                            dve.wait_ge(s_th, tanh_no(pl, pn) + 1)
                            signal(dve.scalar_tensor_tensor(hq[:], ta_, 1.0, zs((N - 1) % 2), ALU.add, ALU.mult), s_hq)
                            dve.wait_ge(s_hq, 4 * pl + pidx + 1)
                        if pkind == "out" and (N - 1) // NC < DEPTH - 1:
                            x_low((N - 1) // NC + 1, pidx, zs((N - 1) % 2))
                    if tick == 2 and pkind == "u":
                        pooling(N - 1)
                    if tick == 3 and pkind == "gate":
                        gate_low(N - 1)
                    if tick % 4 == 2 and N + 1 < NTOT:
                        w_low(N + 1, tick // 4)
                    if tick == 5 and pkind in ("k", "q"):
                        rope_first(N - 1)
                    if tick == MINI_TICK + 1 and n in MINI:
                        mini_out(N)
                    at = att_at(layer, n, tick, 8)
                    if at and at[1] == 0:
                        att_meta(layer, at[0])
                    at = att_at(layer, n, tick, 0)
                    if at:
                        att_mask_max(layer, *at)
                    at = att_at(layer, n, tick, 9)
                    if at and at[1] == 0:
                        att_normalise(layer, at[0])
                    at = att_at(layer, n, tick, 11)
                    if at and at[1] == 0 and ATT_B[layer][at[0]][2] == 1:
                        att_out(layer, at[0])
                    if kind_slot(n) == ("hgrn", 0):
                        H = 4 * layer + (n - 21) // 3
                        if tick == 0:
                            hgrn_prepare(layer, H % 4)
                        if tick % 2 == 1:
                            hgrn_level_out(layer, H, tick // 2)
                    if kind_slot(n) == ("hgrn", 1):
                        H = 4 * layer + (n - 22) // 3
                        if tick == 4:
                            hgrn_states(H)
                        if tick == 6:
                            hgrn_take_out(H)
                        if tick == 15:
                            hgrn_norm(layer, H)
            take_out(NTOT - 1)


def columns():
    sizes = (HA * P, HA * P, HA * P, HA * P, HB * DH, 2 * DH, 2 * DH, HB * DH, NG * P, NG * P)
    at = np.concatenate([[0], np.cumsum(sizes)])
    qa, fa, ia, ga, qb, kb, vb, gb, uc, gc = (int(a) for a in at[:-1])

    def pair(start, i):
        return np.concatenate([start + DH * i + np.arange(DH), start + DH * (i + GRP) + np.arange(DH)])

    def run(start, i):
        return start + P * i + np.arange(P)

    cols = []
    for kind, i in IN_CHUNKS:
        if kind == "gate":
            cols.append(run(ga, i) if i < 4 else pair(gb, i - 4) if i < 12 else run(gc, i - 12))
        else:
            cols.append({"k": lambda: run(kb, 0), "v": lambda: run(vb, 0), "q": lambda: pair(qb, i),
                         "u": lambda: run(uc, i), "hf": lambda: run(fa, i), "hq": lambda: run(qa, i),
                         "hi": lambda: run(ia, i)}[kind]())
    rows = [run(0, i) if i < 4 else pair(HA * P, i - 4) if i < 12 else run(0, i) for i in GATES]
    return np.concatenate(cols), np.concatenate(rows)


def constants():
    f = np.float32
    eye, ones = np.eye(P, dtype=f), np.ones((P, P), f)
    bones = np.kron(np.eye(2, dtype=f), np.ones((DH, DH), f))
    q, k = np.arange(P)[:, None], np.arange(P)[None, :]
    mask = np.zeros((P, 272), f)
    mask[:, 0:P] = np.where(k > q, 0.0, NEG)
    mask[:, P:2 * P] = np.where(k <= q, 0.0, NEG)
    recips = np.stack([1.0 / np.minimum(np.arange(PAD) + 1, w) for w in WINDOWS]).astype(f)
    recips = np.broadcast_to(recips.reshape(1, -1), (P, NG * PAD))
    c_f32 = np.ascontiguousarray(np.concatenate([eye, ones, bones, mask, recips], axis=1))
    inv = np.power(f(10000.0), -np.arange(DH // 2, dtype=f) * f(2.0) / f(DH)).astype(f)
    ang = (np.arange(T, dtype=f)[None, :] * inv[:, None]).astype(f)
    cos, sin = np.cos(ang).astype(f), np.sin(ang).astype(f)
    c_rope = np.ascontiguousarray(np.stack([np.concatenate([cos] * 4), np.concatenate([-sin, sin] * 2)], axis=1))
    lm = np.zeros((P, len(LEVELS), 64), f)
    for l, s in enumerate(LEVELS):
        i = np.arange(64)
        g = i // s
        j = np.arange(P)[:, None]
        m = (j // (2 * s) == g[None, :]) & (j % (2 * s) < s)
        lm[:, l] = m
    return c_rope, c_f32, np.ascontiguousarray(lm.reshape(P, -1))


def kernel(**inputs):
    import concourse.bacc as bacc
    from concourse.bass_utils import run_bass_kernel_spmd

    a = {k: np.asarray(v) for k, v in inputs.items()}
    cols, rows = columns()
    xT = np.concatenate([a["meta_tokens"], a["x"][0]], axis=0).T.reshape(KC, P, T).transpose(1, 0, 2)
    w_in = a["w_in"].reshape(DEPTH, KC, P, -1)[..., cols].reshape(DEPTH, KC, P, N_IN, P)
    w_in = w_in.transpose(0, 3, 2, 1, 4).reshape(DEPTH, N_IN, P, KC * P)
    w_out = a["w_out"][:, rows].reshape(DEPTH, KC, P, KC, P).transpose(0, 3, 2, 1, 4).reshape(DEPTH, KC, P, KC * P)

    prm = []
    for layer in range(DEPTH):
        def col(v):
            return v.reshape(-1, P).T

        def twice(v):
            return np.concatenate([v, v])[:, None]

        qg, kg = a["q_norm_g"][layer], a["k_norm_g"][layer]
        half = DH // 2
        swap = np.concatenate([np.arange(half, DH), np.arange(half)])
        prm.append(np.concatenate([
            col(a["norm_g"][layer]), twice(qg), twice(qg[swap]), twice(kg), twice(kg[swap]),
            a["hgrn_norm_g"][layer][:, None], col(a["pool_scale"][layer]),
            col(a["lb_logits"][0]), col(a["lb_logits"][1]),
            np.broadcast_to(a["attn_sinks"][layer][None, :], (P, HB))], axis=1))
    prm = np.stack(prm, axis=1)
    pool_w = a["pool_w"].transpose(2, 0, 1, 3).reshape(P, DEPTH, NG * P)
    c_rope, c_f32, c_mask = constants()

    nc = bacc.Bacc("TRN2", target_bir_lowering=False, num_devices=1)
    arrays, args = {}, []
    for name, v in (("xT", xT), ("w_in", w_in), ("w_out", w_out), ("prm", prm), ("pool_w", pool_w),
                    ("c_rope", c_rope), ("c_f32", c_f32), ("c_mask", c_mask)):
        v = np.ascontiguousarray(v)
        arrays[f"in_{name}"] = v
        args.append(nc.dram_tensor(f"in_{name}", v.shape, mybir.dt.from_np(v.dtype), kind="ExternalInput").ap())
    outT = nc.dram_tensor("out_0", [KC, P, SEQ], F32, kind="ExternalOutput").ap()
    h1T = nc.dram_tensor("h1T", [KC, P, T], F32, kind="Internal").ap()
    build(nc, *args, outT, h1T)
    r = run_bass_kernel_spmd(nc, [arrays], core_ids=[0])
    got = r.results[0]["out_0"]
    return np.ascontiguousarray(got.reshape(D_MODEL, SEQ).T)[None]
```

```python
from contextlib import ExitStack

import numpy as np

import concourse.bass as bass
from concourse import mybir

F32 = mybir.dt.float32
F32R = mybir.dt.float32r
U8 = mybir.dt.uint8
ACT = mybir.ActivationFunctionType
ALU = mybir.AluOpType

P = 128
DEPTH = 2
D_MODEL = 2048
N_META = 16
SEQ = 512
T = N_META + SEQ
KC = D_MODEL // P
HA = 4
HB = 16
DH = 64
GRP = 8
NG = 4
WINDOWS = (2, 4, 8, 16)
NBLK = SEQ // P
EPS = 1e-6
LOG_FLOOR = 1e-30
NEG = -1e30
PAD = 16

IN_CHUNKS = ([("k", 0), ("v", 0)] + [("q", i) for i in range(8)] + [("u", g) for g in range(NG)]
             + [("gate", 12 + g) for g in range(NG)]
             + [(kind, h) for h in range(HA) for kind in ("hf", "hq", "hi")]
             + [("gate", m) for m in (8, 9, 10, 11, 4, 5, 6, 7, 0, 1, 2, 3)])
N_IN = len(IN_CHUNKS)
CHUNKS = IN_CHUNKS + [("out", c) for c in range(KC)]
NC = len(CHUNKS)
NTOT = DEPTH * NC
GATES = [m for kind, m in IN_CHUNKS if kind == "gate"]
TICKS = KC
HI_TICKS = (2, 5, 8, 11)

MINI = {0: ("rms", 0), 1: ("rope", 0)}
MINI.update({3 + i: ("rope", 1 + i) for i in range(8)})
MINI.update({11 + g: ("pool", g) for g in range(NG)})
MINI.update({23 + 3 * h: ("hnorm", h) for h in range(HA)})
MINI_SLOTS = sorted(MINI)
NORM_SLOTS = [n for n in MINI_SLOTS if MINI[n][0] != "pool"]


def mini_tick(layer, n):
    return 13 if (layer, n) == (0, 0) else 8


ROPE_CHUNKS = [0] + list(range(2, 10))
NROPE = len(ROPE_CHUNKS)
TANH_CHUNKS = [n for n, (kind, _) in enumerate(IN_CHUNKS) if kind in ("gate", "hq")]

C_NORM, C_QG, C_QGS, C_KG, C_KGS, C_HG, C_PS, C_LB, C_SINK, NPRM = 0, 16, 17, 18, 19, 20, 21, 25, 33, 49

ATT_SLOT, ATT_TICK, ATT_LEAD = 11, 2, 4


def att_job(n, tick):
    at = (n - ATT_SLOT) * TICKS + tick - ATT_TICK
    if at < 0 or (at and at * 5 // 8 == (at - 1) * 5 // 8):
        return None
    return at * 5 // 8



def att_batches(layer):
    first = 0 if layer == 0 else 1
    return [(b, j, kv) for b in range(first, NBLK + 1) for j in range(2) for kv in range(2)]


ATT_B = [att_batches(l) for l in range(DEPTH)]
ATT_Q0 = [0, len(ATT_B[0])]


def pairs_before(layer, q):
    return 2 * (sum(b > 0 for b, _, _ in ATT_B[0]) * layer + sum(b > 0 for b, _, _ in ATT_B[layer][:q]))


def hgrn_at(n, tick):
    h, r = divmod((n - 21) * TICKS + tick, 3 * TICKS)
    return (h, r) if 0 <= h < HA else (0, -1)


H_V_T, H_LEVEL, H_K_T, H_INC, H_STATE, H_OUT, H_SQ, H_NORM = 3, 4, 29, 31, 32, 34, 36, 46


def span(layer, n):
    kind = CHUNKS[n][0]
    return (N_META, SEQ // 2) if layer == DEPTH - 1 and kind in ("q", "gate", "out") else (0, T // 2)


def blk(b):
    return slice(0, N_META) if b == 0 else slice(N_META + P * (b - 1), N_META + P * b)


LEVELS = [1, 2, 4, 8, 16, 32, 64]
TAIL = T - 4 * P


def level_cols(s):
    return T if 2 * s <= TAIL else 4 * P


def build(nc, xT, w_in, w_out, prm, pool_w, c_rope, c_f32, c_mask, outT, h1T):
    ctx = ExitStack()
    with ctx:
        top = [0]
        base = -(-nc.sbuf_base // 64) * 64

        def place(name, shape, dt, at=None):
            size = int(np.prod(shape[1:])) * (1 if dt == U8 else 4)
            size = -(-size // 32) * 32
            if at is None:
                at = base + top[0]
                top[0] += size
                assert at + size <= nc.sbuf_usable_end, (name, at + size, nc.sbuf_usable_end)
            return nc.alloc_sbuf_tensor_at(name, shape, dt, offset=at), at + size

        U = T * 4
        xh, _ = place("x_hi", [P, KC, T], F32R)
        xl, _ = place("x_lo", [P, KC, T], F32R)
        mh_at = base + top[0]
        mh, _ = place("mixed_hi", [P, KC, T], F32R)
        ml_at = base + top[0]
        ml, _ = place("mixed_lo", [P, KC, T], F32R)
        wst, _ = place("w_stage", [P, 2, KC, P], F32)
        wh, _ = place("w_hi", [P, 2, KC, P], F32R)
        wl, _ = place("w_lo", [P, 2, KC, P], F32R)
        rstd, _ = place("rstd", [P, T], F32)
        prm_sb, _ = place("prm_sb", [P, DEPTH, NPRM], F32)
        pw_sb, _ = place("pool_w_sb", [P, DEPTH, NG, P], F32)
        cst, _ = place("cst", [P, 3 * P + 272 + NG * PAD], F32)
        lmask, _ = place("level_mask", [P, len(LEVELS), 4, 64], U8)
        lmask_f, _ = place("level_mask_f32", [P, len(LEVELS), 64], F32, ml_at)
        epsc, _ = place("eps_col", [P, 1], F32)
        coef, _ = place("hgrn_coef", [P, DEPTH, 4, HA], F32)
        lbt, _ = place("lb_tmp", [P, 8, HA], F32)
        stat, _ = place("att_stat", [P, 5, 4, 4], F32)
        z, _ = place("z", [P, 2, PAD + T], F32)
        ta, _ = place("ta", [P, PAD + T], F32)
        tb, _ = place("tb", [P, PAD + T], F32)
        th_at = base + top[0]
        th, _ = place("h_tanh", [P, T], F32)
        vt_at = base + top[0]
        vt, _ = place("h_vt", [P, T], F32)
        vh, _ = place("h_v", [P, 5, P], F32)
        pmt, _ = place("a_pmt", [P, P], F32)
        pmc, _ = place("a_pmeta", [P, 2, 4, N_META], F32)
        kt, _ = place("a_kt", [P, T], F32, th_at)
        qs = [place("a_q_stack0", [P, 8, P], F32R, vt_at)[0], place("a_q_stack1", [P, 8, P], F32R, mh_at)[0]]
        res = [place("res0", [P, T], F32, th_at)[0], place("res1", [P, T], F32, vt_at)[0]]

        y, _ = place("y", [P, KC, T], F32, ml_at)
        pts, a1 = place("a_pt", [P, 2, 2, 2, P], F32, ml_at)
        vm, a1 = place("a_vmeta", [P, 2, 4, DH], F32, a1)
        on, a1 = place("a_on", [P, 4, 2, DH], F32, a1)
        assert a1 <= ml_at + 4 * U
        kh, a2 = place("a_k_hi", [P, 2, T], F32R, mh_at + 2 * U)
        kl, a2 = place("a_k_lo", [P, 2, T], F32R, a2)
        vb, a2 = place("a_v", [P, NBLK + 1, P], F32, a2)
        pr, a2 = place("a_p", [P, 2, 4, 272], F32, a2)
        assert a2 <= mh_at + 12 * U
        rope, a3 = place("rope", [P, 2, T], F32, mh_at)
        hf, a3 = place("h_f", [P, T], F32, mh_at)
        hk, a3 = place("h_k", [P, T], F32, a3)
        hq, a3 = place("h_q", [P, T], F32, a3)
        hp, a3 = place("h_qp", [P, T], F32, a3)
        tt, a3 = place("h_tot", [P, T], F32, a3)
        am, a3 = place("h_att", [P, 4, P], F32, a3)
        amt, a3 = place("h_att_tail", [P, TAIL], F32, a3)
        kn, a3 = place("h_kn", [P, 4, P], F32, a3)
        st, a3 = place("h_state", [P, 4, P], F32, a3)
        assert a3 <= mh_at + 8 * U
        xin, _ = place("x_in", [P, KC, T], F32, mh_at)

        eye, ones, bones = cst[:, 0:P], cst[:, P:2 * P], cst[:, 2 * P:3 * P]
        amask = cst[:, 3 * P:3 * P + 272]
        recips = cst[:, 3 * P + 272:3 * P + 272 + NG * PAD].rearrange("p (g t) -> p g t", g=NG)
        st_mx, st_neg, st_den, st_es, st_rd = (stat[:, i] for i in range(5))

        G = ctx.enter_context(nc.psum_tensor("ps_gemm", [P, 2, 2, 512], F32))
        M = ctx.enter_context(nc.psum_tensor("ps_mix", [P, 4, 512], F32))

        def sem(name):
            return ctx.enter_context(nc.semaphore(name))

        s_prm, s_prm0, s_rope = sem("const_in"), sem("prm_in"), sem("rope_in")
        s_x = [sem(f"x_in{q}") for q in range(4)]
        s_w = [sem("w_in0"), sem("w_in1")]
        s_whi, s_wlo, s_gemm, s_z = sem("w_hi_done"), sem("w_lo_done"), sem("gemm_done"), sem("z_done")
        s_mini, s_pevac = sem("mini_done"), sem("pool_evac")
        s_sq, s_swap, s_ln, s_rt, s_ropeo = (sem("square_done"), sem("swap_done"), sem("log_done"),
                                             sem("rsqrt_done"), sem("rope_done"))
        s_kh, s_kl, s_qh, s_ql = sem("a_k_hi_done"), sem("a_k_lo_done"), sem("a_q_hi_done"), sem("a_q_lo_done")
        s_amt, s_ame = sem("a_pmeta_ps"), sem("a_pmeta_sb")
        s_th, s_thf, s_prod, s_mhi, s_mlo = (sem("tanh_done"), sem("tanh_f_done"), sem("prod_done"),
                                             sem("mixed_hi_done"), sem("mixed_lo_done"))
        s_pool = sem("pooled_done")
        s_avt, s_avb, s_avz, s_avm = sem("a_v_t"), sem("a_v_sb"), sem("a_vmeta_zero"), sem("a_vmeta_in")
        s_asc, s_amx, s_aneg, s_aex, s_aes = (sem("a_scores"), sem("a_masked"), sem("a_negmax"),
                                              sem("a_exp"), sem("a_expsink"))
        s_apt, s_ape, s_apv, s_aoe, s_aot, s_aod, s_apm = (sem("a_pt_ps"), sem("a_pt_sb"), sem("a_pv"),
                                                    sem("a_o_norm"), sem("a_o_t"), sem("a_o_done"), sem("a_pmeta_c"))
        s_hq, s_hk, s_hvt, s_hve = sem("h_q_done"), sem("h_k_done"), sem("h_vt_ps"), sem("h_v_sb")
        s_hl, s_hu, s_hkt, s_hke = sem("h_level"), sem("h_update"), sem("h_kt_ps"), sem("h_kt_sb")
        s_hinc, s_hs, s_ho, s_hoe, s_hsq, s_hy = (sem("h_inc"), sem("h_states"), sem("h_o_ps"),
                                                  sem("h_o_sb"), sem("h_o_sq"), sem("h_y_done"))
        s_xhi, s_xsq, s_xlo, s_ss = sem("x_hi_done"), sem("x_sq_done"), sem("x_lo_done"), sem("x_ss_done")
        s_res = [sem("res_in0"), sem("res_in1")]
        s_sto = [sem("store0"), sem("store1")]
        s_lb, s_eps = sem("lb_step"), sem("eps_done")
        s_v, s_a = sem("vector_link"), sem("scalar_link")

        def parts(c0, w):
            return [(0, c0, 2 * w)] if 2 * w <= 512 else [(0, c0, w), (1, c0 + w, w)]

        def halves(ap, c0, w):
            return ap[:, c0:c0 + 2 * w] if 2 * w <= 512 else \
                ap[:, c0:c0 + 2 * w].rearrange("p (a t) -> p a t", a=2)

        def banks(slot, w):
            return G[:, slot, 0, 0:2 * w] if 2 * w <= 512 else G[:, slot, :, 0:w]

        def zs(par):
            return z[:, par, PAD:PAD + T]

        ta_, tb_ = ta[:, PAD:PAD + T], tb[:, PAD:PAD + T]

        def mini_no(layer, n):
            return layer * len(MINI_SLOTS) + MINI_SLOTS.index(n)

        def norm_no(layer, n):
            return layer * len(NORM_SLOTS) + NORM_SLOTS.index(n)

        def pool_no(layer, g):
            return layer * NG + g

        def tanh_no(layer, n):
            return layer * len(TANH_CHUNKS) + TANH_CHUNKS.index(n)

        def att_at(layer, n, tick, lag):
            job = att_job(n, tick)
            if job is None:
                return None
            q, i = divmod(job - ATT_LEAD - lag, 4)
            return (q, i) if 0 <= q < len(ATT_B[layer]) else None

        def store(sp, layer, n):
            c = n - N_IN
            N = NC * layer + n
            sp.wait_ge(s_z, N + 1)
            if layer < DEPTH - 1:
                sp.dma_start(h1T[c], zs(N % 2)).then_inc(s_sto[N % 2], 16)
            else:
                sp.dma_start(outT[c], z[:, N % 2, PAD + N_META:PAD + T]).then_inc(s_sto[N % 2], 16)

        def att_pair_at(layer, n, tick, job):
            now = att_job(n, tick)
            if now is None:
                return None
            m, r = divmod(now - job, 8)
            return m if r == 0 and 0 <= m < len(ATT_B[layer]) // 2 else None

        block = ctx.enter_context(nc.Block())

        @block.sync
        def _(sp):
            def load_w(N):
                if N >= 2:
                    sp.wait_ge(s_wlo, 4 * (N - 1))
                layer, n = divmod(N, NC)
                src = w_in[layer, n] if n < N_IN else w_out[layer, n - N_IN]
                sp.dma_start(wst[:, N % 2].rearrange("p k c -> p (k c)"), src).then_inc(s_w[N % 2], 16)

            def load_x(q):
                sp.dma_start(xin[:, 4 * q:4 * q + 4], xT[:, 4 * q:4 * q + 4]).then_inc(s_x[q], 16)

            sp.dma_start(prm_sb[:], prm).then_inc(s_prm0, 16)
            load_x(0)
            load_w(0)
            for q in range(1, 4):
                load_x(q)
            sp.dma_start(pw_sb[:].rearrange("p l g c -> p l (g c)"), pool_w).then_inc(s_prm, 16)
            sp.dma_start(cst[:], c_f32).then_inc(s_prm, 16)
            sp.dma_start(lmask_f[:].rearrange("p l i -> p (l i)"), c_mask).then_inc(s_prm, 16)
            load_w(1)
            for N in range(NTOT):
                layer, n = divmod(N, NC)
                if N + 2 < NTOT:
                    load_w(N + 2)
                if n == 0:
                    sp.wait_ge(s_xlo, 16)
                    sp.wait_ge(s_xsq, 16)
                    if layer:
                        sp.wait_ge(s_gemm, NC * layer)
                    sp.dma_start(rope[:], c_rope).then_inc(s_rope, 16)
                if n == 2:
                    sp.wait_ge(s_avb, 2 * layer + 2)
                    sp.wait_ge(s_avz, layer + 1)
                    for i in range(4):
                        sp.dma_start(vm[16 * i:16 * i + 16, :, i, :],
                                     vb[0:N_META, 0, :].rearrange("p (v d) -> p v d", v=2)).then_inc(s_avm, 16)
                if n >= N_IN - 1:
                    c = n - (N_IN - 1)
                    if c < KC:
                        if c < 2:
                            sp.wait_ge(s_hy, 4 * (layer + 1))
                        else:
                            sp.wait_ge(s_z, NC * layer + N_IN + c - 1)
                        if layer and c == 0:
                            for par in range(2):
                                sp.wait_ge(s_sto[par], 16 * (KC // 2))
                        src = xT[:, c] if layer == 0 else h1T[c]
                        sp.dma_start(res[c % 2][:], src).then_inc(s_res[c % 2], 16)
                if n > N_IN:
                    store(sp, layer, n - 1)
                if n == 0 and layer:
                    store(sp, layer - 1, NC - 1)
            store(sp, DEPTH - 1, NC - 1)
            for par in range(2):
                sp.wait_ge(s_sto[par], 16 * (KC // 2) * DEPTH)

        @block.gpsimd
        def _(pool):
            for layer in range(DEPTH):
                if layer:
                    pool.wait_ge(s_gemm, NC * layer)
                else:
                    pool.wait_ge(s_xlo, 16)
                    pool.wait_ge(s_xsq, 16)
                pool.memset(vm[:], 0.0).then_inc(s_avz, 1)

        @block.scalar
        def _(act):
            def w_high(N, q):
                if q == 0:
                    act.wait_ge(s_w[N % 2], 16 * (N // 2 + 1))
                    if N >= 2:
                        act.wait_ge(s_gemm, N - 1)
                act.activation(wh[:, N % 2, 4 * q:4 * q + 4], wst[:, N % 2, 4 * q:4 * q + 4], ACT.Copy)\
                   .then_inc(s_whi, 1)

            def x_split(layer, k, src):
                g = prm_sb[:, layer, C_NORM + k:C_NORM + k + 1]
                act.activation(xh[:, k], src, ACT.Copy, scale=g).then_inc(s_xhi, 1)
                if 16 * layer + k:
                    act.wait_ge(s_ss, 16 * layer + k)
                act.activation(ta_, src, ACT.Square).then_inc(s_xsq, 1)

            act.wait_ge(s_prm0, 16)
            act.wait_ge(s_eps, 1)
            act.wait_ge(s_lb, 1)
            act.activation(lbt[:, 2:4], lbt[:, 0:2], ACT.Exp).then_inc(s_lb, 1)
            for k in range(KC):
                if k % 4 == 0:
                    act.wait_ge(s_x[k // 4], 16)
                x_split(0, k, xin[:, k])
                if k % 2 == 1 and k < 8:
                    w_high(0, k // 2)

            for N in range(NTOT):
                layer, n = divmod(N, NC)
                for tick in range(TICKS):
                    if tick == 0 and N:
                        pl, pn = divmod(N - 1, NC)
                        kind, idx = CHUNKS[pn]
                        zz = zs((N - 1) % 2)
                        c0, w = span(pl, pn)
                        cols = slice(c0, c0 + 2 * w)
                        act.wait_ge(s_z, N)
                        if kind in ("k", "q"):
                            R = NROPE * layer + ROPE_CHUNKS.index(pn)
                            if R:
                                act.wait_ge(s_ropeo, R)
                            act.activation(ta_[:, cols], zz[:, cols], ACT.Square).then_inc(s_sq, 1)
                            for quarter in range(4):
                                a, b = 32 * quarter, 32 * (quarter ^ 1)
                                act.activation(tb[a:a + 32, PAD + c0:PAD + c0 + 2 * w],
                                               z[b:b + 32, (N - 1) % 2, PAD + c0:PAD + c0 + 2 * w], ACT.Copy)\
                                   .then_inc(s_swap, 1)
                        elif kind in ("gate", "hq"):
                            act.activation(ta_[:, cols], zz[:, cols], ACT.Tanh, scale=0.5).then_inc(s_th, 1)
                        elif kind == "hf":
                            if 4 * pl + idx:
                                act.wait_ge(s_hk, 4 * pl + idx)
                            act.activation(th[:], zz, ACT.Tanh, scale=0.5).then_inc(s_thf, 1)
                        elif kind == "out" and pl < DEPTH - 1:
                            x_split(pl + 1, idx, zz)
                    if tick in HI_TICKS and N + 1 < NTOT:
                        w_high(N + 1, HI_TICKS.index(tick))
                    if tick == 3 and N and CHUNKS[(N - 1) % NC][0] == "gate":
                        pl, pn = divmod(N - 1, NC)
                        gno = len(GATES) * pl + GATES.index(CHUNKS[pn][1])
                        c0, w = span(pl, pn)
                        act.wait_ge(s_prod, gno + 1)
                        m = CHUNKS[pn][1]
                        act.activation(mh[:, m, c0:c0 + 2 * w], zs((N - 1) % 2)[:, c0:c0 + 2 * w], ACT.Copy)\
                           .then_inc(s_mhi, 1)
                    if n in NORM_SLOTS and tick == mini_tick(layer, n) + 1:
                        kind, idx = MINI[n]
                        no = norm_no(layer, n)
                        act.wait_ge(s_mini, mini_no(layer, n) + 1)
                        buf, size = {"rms": (rstd, D_MODEL), "rope": (ta_, DH), "hnorm": (tb_, P)}[kind]
                        c0, w = span(layer, n - 1) if kind == "rope" else (0, T // 2)
                        src = M[:, 0:2, 0:w] if kind == "rms" else banks((N + 1) % 2, w)
                        act.activation(halves(buf, c0, w), src, ACT.Ln, scale=1.0 / size,
                                       bias=epsc[:, 0:1]).then_inc(s_ln, 1)
                        act.wait_ge(s_ln, no + 1)
                        act.activation(buf[:, c0:c0 + 2 * w], buf[:, c0:c0 + 2 * w], ACT.Exp, scale=-0.5)\
                           .then_inc(s_rt, 1)
                    if n == 3 and tick == 12:
                        act.wait_ge(s_ropeo, NROPE * layer + 1)
                        for kv in range(2):
                            for half in range(2):
                                act.activation(kh[64 * half:64 * half + 64, kv], kt[64 * kv:64 * kv + 64], ACT.Copy)\
                                   .then_inc(s_kh, 1)
                    m = att_pair_at(layer, n, tick, 0)
                    if m is not None:
                        b, j, _ = ATT_B[layer][2 * m]
                        MM = ATT_Q0[layer] // 2 + m
                        nq = N_META if b == 0 else P
                        act.wait_ge(s_ropeo, NROPE * (layer + 1))
                        if MM >= 2:
                            act.wait_ge(s_asc, 8 * (MM - 1))
                        for kv in range(2):
                            rows = slice(64 * kv, 64 * kv + 64)
                            act.activation(qs[MM % 2][rows, 4 * kv:4 * kv + 4, 0:nq],
                                           y[rows, 4 + 4 * j:8 + 4 * j, blk(b)], ACT.Copy).then_inc(s_qh, 1)
                    if n == 2 and tick == 2:
                        act.wait_ge(s_avt, layer + 1)
                        act.activation(vb[:, 1:NBLK + 1], M[:, 0].rearrange("p (b c) -> p b c", b=NBLK), ACT.Copy)\
                           .then_inc(s_avb, 1)
                        act.activation(vb[0:N_META, 0], M[0:N_META, 1, 0:P], ACT.Copy).then_inc(s_avb, 1)
                    at = att_at(layer, n, tick, 4)
                    if at:
                        q, i = at
                        Q = ATT_Q0[layer] + q
                        b = ATT_B[layer][q][0]
                        nq = N_META if b == 0 else P
                        lo = (256, 128, 0)[min(b, 2)]
                        if i == 0:
                            act.wait_ge(s_aneg, Q + 1)
                            act.activation(st_es[0:nq, Q % 4], st_es[0:nq, Q % 4], ACT.Exp).then_inc(s_aes, 1)
                        act.activation(pr[0:nq, Q % 2, i, lo:272], pr[0:nq, Q % 2, i, lo:272], ACT.Exp,
                                       bias=st_neg[0:nq, Q % 4, i:i + 1],
                                       accum_out=st_den[0:nq, Q % 4, i:i + 1]).then_inc(s_aex, 1)
                    at = att_at(layer, n, tick, 5)
                    if at and at[1] % 2 == 1 and ATT_B[layer][at[0]][0]:
                        q, i = at
                        Q = ATT_Q0[layer] + q
                        first = 0 if ATT_B[layer][q][0] >= 2 else 1
                        act.wait_ge(s_apt, pairs_before(layer, q) + i // 2 + 1)
                        if Q:
                            act.wait_ge(s_apv, Q)
                        act.activation(pts[:, i // 2, :, first:2],
                                       M[:, 2].rearrange("p (i s q) -> p i s q", i=2, s=2)[:, :, first:2], ACT.Copy)\
                           .then_inc(s_ape, 1)
                    at = att_at(layer, n, tick, 9)
                    if at and at[1] == 0:
                        Q = ATT_Q0[layer] + at[0]
                        nq = N_META if ATT_B[layer][at[0]][0] == 0 else P
                        act.wait_ge(s_amt, Q + 1)
                        act.activation(pmt[0:64, 0:nq], M[0:64, 3, 0:nq], ACT.Copy).then_inc(s_ame, 1)
                    h, r = hgrn_at(n, tick)
                    H = 4 * layer + h
                    if r >= 0:
                        if r == H_V_T + 1:
                            act.wait_ge(s_hvt, H + 1)
                            if H:
                                act.wait_ge(s_ho, H)
                            act.activation(vh[:, 0:4], M[:, 3].rearrange("p (b c) -> p b c", b=4), ACT.Copy)\
                               .then_inc(s_hve, 1)
                            act.activation(vh[0:TAIL, 4], M[0:TAIL, 2, 0:P], ACT.Copy).then_inc(s_hve, 1)
                    if r >= 0:
                        if r == H_K_T + 1:
                            act.wait_ge(s_hkt, H + 1)
                            act.activation(kn[:], M[:, 0].rearrange("p (b c) -> p b c", b=4), ACT.Copy)\
                               .then_inc(s_hke, 1)
                        if r == H_SQ:
                            act.wait_ge(s_hoe, H + 1)
                            act.activation(tb_, y[:, H % 4], ACT.Square).then_inc(s_hsq, 1)

        @block.tensor
        def _(pe):
            def mini(N, layer, n):
                kind, idx = MINI[n]
                no = mini_no(layer, n)
                g = M if kind == "rms" else G[:, (N + 1) % 2]
                c0, w = (0, T // 2)
                if kind == "rms":
                    if layer:
                        pe.wait_ge(s_hs, 4 * layer)
                elif N:
                    pe.wait_ge(s_z, N)
                if kind == "rms":
                    pe.wait_ge(s_ss, 16 * layer + 16)
                    lhs, rhs = ones, rstd
                elif kind == "rope":
                    c0, w = span(layer, n - 1)
                    pe.wait_ge(s_sq, NROPE * layer + idx + 1)
                    lhs, rhs = bones, ta_
                elif kind == "pool":
                    pe.wait_ge(s_pool, NG * layer + idx + 1)
                    lhs, rhs = pw_sb[:, layer, idx], ta_
                else:
                    pe.wait_ge(s_hsq, 4 * layer + idx + 1)
                    lhs, rhs = ones, tb_
                for bank, c, size in parts(c0, w):
                    ins = pe.matmul(g[:, bank, 0:size], lhs, rhs[:, c:c + size], start=True, stop=True)
                ins.then_inc(s_mini, 1)

            def scores(layer, q, i):
                Q = ATT_Q0[layer] + q
                b, j, kv = ATT_B[layer][q]
                J = 4 * Q + i
                MM = Q // 2
                nq = N_META if b == 0 else P
                if i == 0 and kv == 0:
                    pe.wait_ge(s_ql, 2 * MM + 2)
                if q == 0 and i == 0:
                    pe.wait_ge(s_kl, 4 * layer + 4)
                    pe.wait_ge(s_avb, 2 * layer + 2)
                if J >= 2:
                    pe.wait_ge(s_amx, J - 1)
                qT = qs[MM % 2][:, 4 * kv + i, 0:nq]
                pieces = [(256, 0, N_META)]
                if b >= 1:
                    lo, first = (P, blk(b).start) if b == 1 else (0, blk(b - 1).start)
                    pieces.insert(0, (lo, first, 256 - lo))
                for at, first, size in pieces:
                    for k_part in (kh, kl):
                        ins = pe.matmul(M[0:nq, J % 2, at:at + size], qT, k_part[:, kv, first:first + size],
                                        start=k_part is kh, stop=k_part is kl)
                ins.then_inc(s_asc, 1)

            def probs_t(layer, q, pair):
                Q = ATT_Q0[layer] + q
                b = ATT_B[layer][q][0]
                no = pairs_before(layer, q) + pair
                pe.wait_ge(s_aex, 4 * Q + 2 * pair + 2)
                if no:
                    pe.wait_ge(s_ape, no)
                for i in range(2):
                    for s in range(0 if b >= 2 else 1, 2):
                        c = P * (2 * i + s)
                        ins = pe.transpose(M[:, 2, c:c + P], pr[:, Q % 2, 2 * pair + i, P * s:P * s + P], eye)
                ins.then_inc(s_apt, 1)

            def probs_meta_t(layer, q):
                Q = ATT_Q0[layer] + q
                nq = N_META if ATT_B[layer][q][0] == 0 else P
                pe.wait_ge(s_apm, Q + 1)
                if Q:
                    pe.wait_ge(s_aoe, Q)
                    pe.wait_ge(s_aod, Q // 2)
                pe.transpose(M[0:64, 3, 0:nq], pmc[0:nq, Q % 2].rearrange("p i k -> p (i k)"), eye[0:nq, 0:nq])\
                  .then_inc(s_amt, 1)

            def values(layer, q):
                Q = ATT_Q0[layer] + q
                b, j, kv = ATT_B[layer][q]
                nq = N_META if b == 0 else P
                pe.wait_ge(s_ame, Q + 1)
                if b:
                    pe.wait_ge(s_ape, pairs_before(layer, q + 1))
                if q == 0:
                    pe.wait_ge(s_avm, 64 * (layer + 1))
                o = M[0:nq, 3, 0:256]
                last = pe.matmul(o, pmt[0:64, 0:nq], vm[0:64, kv].rearrange("p i d -> p (i d)"),
                                 start=True, stop=b == 0)
                if b:
                    for i in range(4):
                        for s in range(0 if b >= 2 else 1, 2):
                            last = pe.matmul(o[:, DH * i:DH * i + DH], pts[:, i // 2, i % 2, s],
                                             vb[:, b - 1 + s, DH * kv:DH * kv + DH],
                                             start=False, stop=i == 3 and s == 1)
                last.then_inc(s_apv, 1)

            def outputs_t(layer, q):
                Q = ATT_Q0[layer] + q
                b = ATT_B[layer][q][0]
                nq = N_META if b == 0 else P
                pe.wait_ge(s_aoe, Q + 1)
                for i in range(4):
                    ins = pe.transpose(M[:, 3, P * i:P * i + nq], on[0:nq, i].rearrange("p v d -> p (v d)"),
                                       eye[0:nq, 0:nq])
                ins.then_inc(s_aot, 1)

            def hgrn_level(layer, H, l):
                bank = M[:, l % 2]
                pe.wait_ge(s_hk, H + 1)
                if l == 0:
                    if H == 4 * layer:
                        pe.wait_ge(s_amx, 4 * (ATT_Q0[layer] + len(ATT_B[layer])))
                    if H:
                        pe.wait_ge(s_hs, H)
                else:
                    pe.wait_ge(s_hu, 8 * H + l)
                for b in range(4):
                    kcols = slice(P * b, P * b + P)
                    if l == 0:
                        ins = pe.matmul(bank[:, kcols], hk[:, kcols], hq[:, kcols], start=True, stop=True)
                    else:
                        s = LEVELS[l - 1]
                        rhs = hp[:, kcols].rearrange("p (g two s) -> p g two s", two=2, s=s)[:, :, 1]
                        ins = pe.matmul(bank[:, 64 * b:64 * b + 64], hk[:, kcols], rhs, start=True, stop=True)
                kcols = slice(4 * P, T)
                if l == 0:
                    ins = pe.matmul(M[0:TAIL, 1, 0:TAIL], hk[:, kcols], hq[:, kcols], start=True, stop=True)
                elif level_cols(LEVELS[l - 1]) == T:
                    s = LEVELS[l - 1]
                    rhs = hp[:, kcols].rearrange("p (g two s) -> p g two s", two=2, s=s)[:, :, 1]
                    ins = pe.matmul(bank[0:TAIL, 256:256 + TAIL // 2], hk[:, kcols], rhs, start=True, stop=True)
                ins.then_inc(s_hl, 1)

            def hgrn_v_t(H):
                pe.wait_ge(s_z, NC * (H // 4) + 21 + 3 * (H % 4))
                if H % 4:
                    pe.wait_ge(s_hoe, H)
                else:
                    pe.wait_ge(s_aod, (ATT_Q0[H // 4] + len(ATT_B[H // 4])) // 2)
                    pe.wait_ge(s_ape, pairs_before(H // 4, len(ATT_B[H // 4])))
                for b in range(4):
                    pe.transpose(M[:, 3, P * b:P * b + P], vt[:, P * b:P * b + P], eye)
                pe.transpose(M[0:TAIL, 2, 0:P], vt[:, 4 * P:T], eye).then_inc(s_hvt, 1)

            def hgrn_k_t(H):
                pe.wait_ge(s_hu, 8 * H + 8)
                for b in range(4):
                    ins = pe.transpose(M[:, 0, P * b:P * b + P], hk[:, P * b:P * b + P], eye)
                ins.then_inc(s_hkt, 1)

            def hgrn_increments(H):
                pe.wait_ge(s_hke, H + 1)
                pe.wait_ge(s_hve, 2 * H + 2)
                for b in range(4):
                    ins = pe.matmul(M[:, 1, P * b:P * b + P], kn[:, b], vh[:, b], start=True, stop=True)
                ins.then_inc(s_hinc, 1)

            def hgrn_out(H):
                pe.wait_ge(s_hs, H + 1)
                for b in range(5):
                    cols = slice(P * b, min(P * b + P, T))
                    o = M[:, 3, cols] if b < 4 else M[:, 2, 0:TAIL]
                    lhs = vh[:, b] if b < 4 else vh[0:TAIL, 4]
                    rhs = am[:, b] if b < 4 else amt[0:TAIL]
                    ins = pe.matmul(o, lhs, rhs, start=True, stop=b == 0)
                    if b:
                        ins = pe.matmul(o, st[:, b - 1], hp[:, cols], start=False, stop=True)
                ins.then_inc(s_ho, 1)

            for N in range(NTOT):
                layer, n = divmod(N, NC)
                g = G[:, N % 2]
                c0, w = span(layer, n)
                if N >= 2:
                    pe.wait_ge(s_z, N - 1)
                pl, pn = divmod(N - 1, NC)
                if N and pn in MINI:
                    if MINI[pn][0] == "rms":
                        pass
                    elif MINI[pn][0] == "pool":
                        pe.wait_ge(s_pevac, pool_no(pl, MINI[pn][1]) + 1)
                    else:
                        pe.wait_ge(s_ln, norm_no(pl, pn) + 1)
                for tick in range(TICKS):
                    k = tick if n < N_IN else GATES[tick]
                    if tick % 4 == 0:
                        pe.wait_ge(s_wlo, 4 * N + tick // 4 + 1)
                    if n == 0:
                        pe.wait_ge(s_xlo, 16 * layer + tick + 1)
                    if n == N_IN:
                        pe.wait_ge(s_mlo, len(GATES) * layer + tick + 1)
                    hi, lo = (xh, xl) if n < N_IN else (mh, ml)
                    passes = ((wh, hi), (wh, lo), (wl, hi))
                    for i, (ws, xs) in enumerate(passes):
                        for bank, c, size in parts(c0, w):
                            ins = pe.matmul(g[:, bank, 0:size], ws[:, N % 2, tick], xs[:, k, c:c + size],
                                            start=tick == 0 and i == 0, stop=tick == TICKS - 1 and i == 2)
                    if tick == TICKS - 1:
                        ins.then_inc(s_gemm, 1)
                    if N == 0 and tick == 12:
                        pe.wait_ge(s_prm, 48)
                    if n in MINI and tick == mini_tick(layer, n):
                        mini(N, layer, n)
                    if n == 2 and tick == 1:
                        pe.wait_ge(s_z, N)
                        pe.wait_ge(s_ln, norm_no(layer, 0) + 1)
                        vz = zs((N - 1) % 2)
                        for b in range(NBLK):
                            pe.transpose(M[:, 0, P * b:P * b + P], vz[:, blk(b + 1)], eye)
                        pe.transpose(M[0:N_META, 1, 0:P], vz[:, 0:N_META], eye).then_inc(s_avt, 1)
                    at = att_at(layer, n, tick, 0)
                    if at:
                        scores(layer, *at)
                    at = att_at(layer, n, tick, 9)
                    if at and at[1] == 0:
                        probs_meta_t(layer, at[0])
                    at = att_at(layer, n, tick, 10)
                    if at and at[1] == 0:
                        values(layer, at[0])
                    at = att_at(layer, n, tick, 5)
                    if at and at[1] % 2 == 1 and ATT_B[layer][at[0]][0]:
                        probs_t(layer, at[0], at[1] // 2)
                    at = att_at(layer, n, tick, 11)
                    if at and at[1] == 0 and ATT_B[layer][at[0]][2] == 1:
                        outputs_t(layer, at[0])
                    h, r = hgrn_at(n, tick)
                    H = 4 * layer + h
                    if r == H_V_T:
                        hgrn_v_t(H)
                    if H_LEVEL <= r < H_LEVEL + 24 and (r - H_LEVEL) % 3 == 0:
                        hgrn_level(layer, H, (r - H_LEVEL) // 3)
                    if r == H_K_T:
                        hgrn_k_t(H)
                    if r == H_INC:
                        hgrn_increments(H)
                    if r == H_OUT:
                        hgrn_out(H)

        @block.vector
        def _(dve):
            links = [0]

            def link(ins):
                links[0] += 1
                ins.then_inc(s_v, 1)
                dve.wait_ge(s_v, links[0])

            counts = {}

            def signal(ins, s):
                counts[s.name] = counts[s.name] + 1 if s.name in counts else 1
                ins.then_inc(s, 1)
                dve.wait_ge(s, counts[s.name])

            def w_low(N, q):
                dve.wait_ge(s_whi, 4 * N + q + 1)
                part = (slice(None), N % 2, slice(4 * q, 4 * q + 4))
                dve.tensor_tensor(wl[part], wst[part], wh[part].bitcast(F32), ALU.subtract).then_inc(s_wlo, 1)

            def x_low(layer, k, src):
                g = prm_sb[:, layer, C_NORM + k:C_NORM + k + 1]
                dve.wait_ge(s_xhi, 16 * layer + k + 1)
                signal(dve.scalar_tensor_tensor(xl[:, k], src, g, xh[:, k].bitcast(F32), ALU.mult, ALU.subtract), s_xlo)
                dve.wait_ge(s_xsq, 16 * layer + k + 1)
                if k == 0:
                    signal(dve.tensor_copy(rstd[:], ta_), s_ss)
                else:
                    dve.wait_ge(s_ss, 16 * layer + k)
                    signal(dve.tensor_tensor(rstd[:], rstd[:], ta_, ALU.add), s_ss)

            link(dve.memset(z[:, :, 0:PAD], 0.0))
            link(dve.memset(ta[:, 0:PAD], 0.0))
            link(dve.memset(tb[:, 0:PAD], 0.0))
            signal(dve.memset(epsc[:], EPS), s_eps)
            dve.wait_ge(s_prm0, 16)
            l0, l1 = prm_sb[:, 0, C_LB:C_LB + HA], prm_sb[:, 0, C_LB + HA:C_LB + 2 * HA]
            link(dve.tensor_tensor(lbt[:, 4], l0, l1, ALU.max))
            link(dve.tensor_tensor(lbt[:, 0], l0, lbt[:, 4], ALU.subtract))
            dve.tensor_tensor(lbt[:, 1], l1, lbt[:, 4], ALU.subtract).then_inc(s_lb, 1)
            for k in range(KC):
                x_low(0, k, xin[:, k])
                if k % 2 == 1 and k < 8:
                    w_low(0, k // 2)
            dve.wait_ge(s_prm, 48)
            for b in range(4):
                link(dve.tensor_copy(lmask[:, :, b], lmask_f[:]))
            dve.wait_ge(s_lb, 2)
            link(dve.tensor_tensor(lbt[:, 4], lbt[:, 2], lbt[:, 3], ALU.add))
            link(dve.reciprocal(lbt[:, 5], lbt[:, 4]))
            link(dve.tensor_tensor(lbt[:, 2], lbt[:, 2], lbt[:, 5], ALU.mult))
            link(dve.tensor_tensor(lbt[:, 3], lbt[:, 3], lbt[:, 5], ALU.mult))
            link(dve.tensor_tensor(lbt[:, 6], lbt[:, 2], lbt[:, 2], ALU.subtract))
            link(dve.tensor_tensor(lbt[:, 7], lbt[:, 2], lbt[:, 3], ALU.add))
            link(dve.tensor_tensor(lbt[:, 7], lbt[:, 7], lbt[:, 2], ALU.subtract))
            for layer in range(DEPTH):
                lb, (a, b, na, ha) = lbt[:, 6 + layer], (coef[:, layer, i] for i in range(4))
                link(dve.tensor_scalar(a, lb, -0.5, 0.5, ALU.mult, ALU.add))
                link(dve.tensor_tensor(b, lb, a, ALU.add))
                link(dve.tensor_scalar(na, a, -0.5, None, ALU.mult))
                link(dve.tensor_scalar(ha, a, 0.5, None, ALU.mult))

            def take_out(N):
                layer, n = divmod(N, NC)
                kind, idx = CHUNKS[n]
                c0, w = span(layer, n)
                zz = zs(N % 2)
                src = banks(N % 2, w)
                dve.wait_ge(s_gemm, N + 1)
                if kind == "out":
                    dve.wait_ge(s_res[idx % 2], 16 * (KC // 2 * layer + idx // 2 + 1))
                    if KC * layer + idx >= 2:
                        dve.wait_ge(s_sto[N % 2], 16 * ((KC * layer + idx) // 2))
                    if layer == DEPTH - 1 and idx == 0:
                        pass
                    signal(dve.tensor_tensor(halves(zz, c0, w), src, halves(res[idx % 2], c0, w), ALU.add), s_z)
                    return
                if layer and n < 2:
                    dve.wait_ge(s_sto[N % 2], 16 * (KC // 2) * layer)
                if n == 0:
                    dve.wait_ge(s_rt, norm_no(layer, 0) + 1)
                dst = zz
                if kind == "hi":
                    dst = vt
                    if 4 * layer + idx:
                        dve.wait_ge(s_hvt, 4 * layer + idx)
                signal(dve.tensor_tensor(halves(dst, c0, w), src, halves(rstd, c0, w), ALU.mult), s_z)

            def rope_first(N):
                layer, n = divmod(N, NC)
                kind = CHUNKS[n][0]
                R = NROPE * layer + ROPE_CHUNKS.index(n)
                c0, w = span(layer, n)
                c = slice(c0, c0 + 2 * w)
                gcol = C_KG if kind == "k" else C_QG
                g, gs = (prm_sb[:, layer, gcol + i:gcol + i + 1] for i in range(2))
                zz = zs(N % 2)
                dve.wait_ge(s_rope, 16 * (layer + 1))
                dve.wait_ge(s_sq, R + 1)
                dve.wait_ge(s_swap, 4 * (R + 1))
                link(dve.scalar_tensor_tensor(tb_[:, c], tb_[:, c], gs, rope[:, 1, c], ALU.mult, ALU.mult))
                link(dve.scalar_tensor_tensor(zz[:, c], zz[:, c], g, rope[:, 0, c], ALU.mult, ALU.mult))
                link(dve.tensor_tensor(zz[:, c], zz[:, c], tb_[:, c], ALU.add))

            def rope_last(N):
                layer, n = divmod(N, NC)
                kind, idx = CHUNKS[n]
                c0, w = span(layer, n)
                c = slice(c0, c0 + 2 * w)
                dve.wait_ge(s_rt, norm_no(layer, n + 1) + 1)
                dst = kt[:, c] if kind == "k" else y[:, 4 + idx, c]
                R = NROPE * layer + ROPE_CHUNKS.index(n)
                signal(dve.tensor_tensor(dst, zs(N % 2)[:, c], ta_[:, c], ALU.mult), s_ropeo)

            def mini_out(N):
                layer, n = divmod(N, NC)
                kind, idx = MINI[n]
                no = mini_no(layer, n)
                dve.wait_ge(s_mini, no + 1)
                c0, w = span(layer, n - 1) if kind == "rope" else (0, T // 2)
                src = banks((N + 1) % 2, w)
                if kind == "pool":
                    signal(dve.tensor_scalar(halves(y[:, 12 + idx], 0, w), src, prm_sb[:, layer, C_PS + idx:C_PS + idx + 1],
                                      None, ALU.mult), s_pevac)
                    return
            def pooling(N):
                layer, n = divmod(N, NC)
                g = CHUNKS[n][1]
                u = z[:, N % 2]
                cur, d = u, 1
                if g == 0:
                    dve.wait_ge(s_ropeo, NROPE * (layer + 1))
                else:
                    dve.wait_ge(s_pevac, pool_no(layer, g - 1) + 1)
                bufs = [ta[:], tb[:]]
                step = 0 if g % 2 == 1 else 1
                while d < WINDOWS[g]:
                    nxt = bufs[step % 2]
                    link(dve.tensor_tensor(nxt[:, PAD:], cur[:, PAD:], cur[:, PAD - d:PAD + T - d], ALU.add))
                    cur, d, step = nxt, 2 * d, step + 1
                link(dve.tensor_tensor(ta[:, PAD:2 * PAD], cur[:, PAD:2 * PAD], recips[:, g], ALU.mult))
                link(dve.tensor_tensor(ta[:, PAD:2 * PAD], ta[:, PAD:2 * PAD], u[:, PAD:2 * PAD], ALU.subtract))
                signal(dve.scalar_tensor_tensor(ta[:, 2 * PAD:], cur[:, 2 * PAD:], 1.0 / WINDOWS[g], u[:, 2 * PAD:],
                                         ALU.mult, ALU.subtract), s_pool)

            def gate_product(N):
                layer, n = divmod(N, NC)
                m = CHUNKS[n][1]
                c0, w = span(layer, n)
                c = slice(c0, c0 + 2 * w)
                zz = zs(N % 2)
                dve.wait_ge(s_th, tanh_no(layer, n) + 1)
                link(dve.scalar_tensor_tensor(zz[:, c], ta_[:, c], 1.0, zz[:, c], ALU.add, ALU.mult))
                if m == 8:
                    dve.wait_ge(s_aod, (ATT_Q0[layer] + len(ATT_B[layer])) // 2)
                if m < HA:
                    dve.wait_ge(s_hy, 4 * layer + m + 1)
                signal(dve.scalar_tensor_tensor(zz[:, c], zz[:, c], 0.5, y[:, m, c], ALU.mult, ALU.mult), s_prod)

            def gate_low(N):
                layer, n = divmod(N, NC)
                m = CHUNKS[n][1]
                c0, w = span(layer, n)
                c = slice(c0, c0 + 2 * w)
                dve.wait_ge(s_mhi, len(GATES) * layer + GATES.index(m) + 1)
                signal(dve.tensor_tensor(ml[:, m, c], zs(N % 2)[:, c], mh[:, m, c].bitcast(F32), ALU.subtract), s_mlo)

            def att_mask_max(layer, q, i):
                Q = ATT_Q0[layer] + q
                b, j, kv = ATT_B[layer][q]
                J = 4 * Q + i
                nq = N_META if b == 0 else P
                lo = (256, 128, 0)[min(b, 2)]
                head = GRP * kv + 4 * j + i
                sink = prm_sb[0:nq, layer, C_SINK + head:C_SINK + head + 1]
                mask = amask[0:nq, P:P + N_META] if b == 0 else amask[:, lo:272]
                dve.wait_ge(s_asc, J + 1)
                if Q >= 2 and i == 0:
                    lq = (layer, q - 2) if q >= 2 else (layer - 1, len(ATT_B[layer - 1]) + q - 2)
                    dve.wait_ge(s_apt, pairs_before(lq[0], lq[1] + 1))
                    dve.wait_ge(s_apm, Q - 1)
                signal(dve.tensor_tensor_reduce(pr[0:nq, Q % 2, i, lo:272], M[0:nq, J % 2, lo:272], mask, DH ** -0.5,
                                         sink, ALU.add, ALU.max, st_mx[0:nq, Q % 4, i:i + 1]), s_amx)
                if i == 3:
                    dve.wait_ge(s_amx, J + 1)
                    link(dve.tensor_scalar(st_neg[0:nq, Q % 4], st_mx[0:nq, Q % 4], -1.0, None, ALU.mult))
                    sinks = prm_sb[0:nq, layer, C_SINK + head - 3:C_SINK + head + 1]
                    signal(dve.tensor_tensor(st_es[0:nq, Q % 4], sinks, st_mx[0:nq, Q % 4], ALU.subtract), s_aneg)

            def att_meta(layer, q):
                Q = ATT_Q0[layer] + q
                nq = N_META if ATT_B[layer][q][0] == 0 else P
                dve.wait_ge(s_aex, 4 * Q + 4)
                if Q >= 2:
                    dve.wait_ge(s_amt, Q - 1)
                signal(dve.tensor_copy(pmc[0:nq, Q % 2], pr[0:nq, Q % 2, :, 256:272]), s_apm)

            def att_normalise(layer, q):
                Q = ATT_Q0[layer] + q
                b, j, kv = ATT_B[layer][q]
                nq = N_META if b == 0 else P
                dve.wait_ge(s_aex, 4 * Q + 4)
                link(dve.tensor_tensor(st_rd[0:nq, Q % 4], st_den[0:nq, Q % 4], st_es[0:nq, Q % 4], ALU.add))
                link(dve.reciprocal(st_rd[0:nq, Q % 4], st_rd[0:nq, Q % 4]))
                dve.wait_ge(s_apv, Q + 1)
                rd = st_rd[0:nq, Q % 4].unsqueeze(2).broadcast_to([nq, 4, DH])
                signal(dve.tensor_tensor(on[0:nq, :, kv], M[0:nq, 3, 0:256]
                                  .rearrange("p (i d) -> p i d", i=4), rd, ALU.mult), s_aoe)

            def att_out(layer, q):
                Q = ATT_Q0[layer] + q
                b, j, kv = ATT_B[layer][q]
                nq = N_META if b == 0 else P
                dve.wait_ge(s_aot, Q // 2 + 1)
                signal(dve.tensor_copy(y[:, 4 + 4 * j:8 + 4 * j, blk(b)],
                                M[:, 3].rearrange("p (i q) -> p i q", i=4)[:, :, 0:nq]), s_aod)

            def hgrn_prepare(layer, h):
                H = 4 * layer + h
                a, b, na, ha = (coef[:, layer, i, h:h + 1] for i in range(4))
                dve.wait_ge(s_thf, H + 1)
                if H:
                    dve.wait_ge(s_ho, H)
                link(dve.tensor_scalar(hf[:], th[:], a, b, ALU.mult, ALU.add))
                link(dve.tensor_scalar(hf[:], hf[:], LOG_FLOOR, None, ALU.max))
                link(dve.tensor_scalar(hk[:], th[:], na, ha, ALU.mult, ALU.add))
                signal(dve.tensor_tensor(hp[:], hq[:], hf[:], ALU.mult), s_hk)
                dve.wait_ge(s_hk, H + 1)

            def hgrn_level_out(layer, H, l):
                dve.wait_ge(s_hl, 8 * H + l + 1)
                bank = M[:, l % 2]
                if l == 0:
                    e4 = eye.unsqueeze(1).broadcast_to([P, 4, P])
                    dve.tensor_tensor(am[:], bank.rearrange("p (b i) -> p b i", b=4), e4, ALU.mult)\
                       .then_inc(s_v, 1)
                    signal(dve.tensor_tensor(amt[0:TAIL], M[0:TAIL, 1, 0:TAIL], eye[0:TAIL, 0:TAIL], ALU.mult), s_hu)
                    links[0] += 1
                    dve.wait_ge(s_v, links[0])
                    dve.wait_ge(s_hu, 8 * H + 1)
                    return
                s = LEVELS[l - 1]
                cols = level_cols(s)
                ng = cols // (2 * s)
                amv = am[:].rearrange("p b i -> p (b i)").rearrange("p (g two s) -> p g two s", two=2, s=s)
                link(dve.copy_predicated(amv[:, :, 1], lmask[:, l - 1].rearrange("p b i -> p (b i)").rearrange("p (g s) -> p g s", s=s),
                                         bank[:, 0:256].rearrange("p (g s) -> p g s", s=s)))
                if cols == T:
                    atv = amt[0:TAIL].rearrange("p (g two s) -> p g two s", two=2, s=s)
                    link(dve.copy_predicated(atv[:, :, 1],
                                             lmask[0:TAIL, l - 1, 0, 0:TAIL // 2].rearrange("p (g s) -> p g s", s=s),
                                             bank[0:TAIL, 256:256 + TAIL // 2].rearrange("p (g s) -> p g s", s=s)))
                off = {1: None, 2: 0, 4: 264, 8: 396, 16: 462, 32: 495, 64: 511, 128: 519}
                cur = hf[:] if s == 1 else tt[:, off[s]:off[s] + 2 * ng]
                pair = cur[:, 0:2 * ng].rearrange("p (g two) -> p g two", two=2)
                qv = hp[:, 0:cols].rearrange("p (g two s) -> p g two s", two=2, s=s)
                kv = hk[:, 0:cols].rearrange("p (g two s) -> p g two s", two=2, s=s)
                link(dve.tensor_tensor(tt[:, off[2 * s]:off[2 * s] + ng], pair[:, :, 0], pair[:, :, 1], ALU.mult))
                link(dve.tensor_tensor(qv[:, :, 1], qv[:, :, 1],
                                       pair[:, :, 0].unsqueeze(2).broadcast_to([P, ng, s]), ALU.mult))
                signal(dve.tensor_tensor(kv[:, :, 0], kv[:, :, 0],
                                  pair[:, :, 1].unsqueeze(2).broadcast_to([P, ng, s]), ALU.mult), s_hu)
                dve.wait_ge(s_hu, 8 * H + l + 1)

            def hgrn_states(H):
                dve.wait_ge(s_hinc, H + 1)
                link(dve.tensor_copy(st[:, 0], M[:, 1, 0:P]))
                for b in range(1, 4):
                    ins = dve.scalar_tensor_tensor(st[:, b], st[:, b - 1], tt[:, 519 + b:520 + b],
                                                   M[:, 1, P * b:P * b + P], ALU.mult, ALU.add)
                    if b < 3:
                        link(ins)
                signal(ins, s_hs)

            def hgrn_take_out(H):
                dve.wait_ge(s_ho, H + 1)
                link(dve.tensor_copy(y[:, H % 4, 0:4 * P], M[:, 3]))
                signal(dve.tensor_copy(y[:, H % 4, 4 * P:T], M[:, 2, 0:TAIL]), s_hoe)

            def hgrn_norm(layer, H):
                dve.wait_ge(s_rt, norm_no(layer, 23 + 3 * (H % 4)) + 1)
                signal(dve.scalar_tensor_tensor(y[:, H % 4], y[:, H % 4], prm_sb[:, layer, C_HG:C_HG + 1], tb_,
                                         ALU.mult, ALU.mult), s_hy)

            for N in range(NTOT):
                layer, n = divmod(N, NC)
                pkind, pidx = CHUNKS[(N - 1) % NC] if N else ("", 0)
                for tick in range(TICKS):
                    if tick == 0 and N:
                        take_out(N - 1)
                    if tick == 1 and N >= 2 and CHUNKS[(N - 2) % NC][0] in ("k", "q"):
                        rope_last(N - 2)
                    if tick == 2 and pkind == "gate":
                        gate_product(N - 1)
                    if tick == 1:
                        if pkind == "hq":
                            pl, pn = divmod(N - 1, NC)
                            dve.wait_ge(s_th, tanh_no(pl, pn) + 1)
                            signal(dve.scalar_tensor_tensor(hq[:], ta_, 1.0, zs((N - 1) % 2), ALU.add, ALU.mult), s_hq)
                        if pkind == "out" and (N - 1) // NC < DEPTH - 1:
                            x_low((N - 1) // NC + 1, pidx, zs((N - 1) % 2))
                    if tick == 2 and pkind == "u":
                        pooling(N - 1)
                    if tick - 1 in HI_TICKS and N + 1 < NTOT:
                        w_low(N + 1, HI_TICKS.index(tick - 1))
                    if tick == 5 and pkind == "gate":
                        gate_low(N - 1)
                    if tick == 5 and pkind in ("k", "q"):
                        rope_first(N - 1)
                    if n in MINI and MINI[n][0] == "pool" and tick == mini_tick(layer, n) + 1:
                        mini_out(N)
                    if n == 3 and tick == 13:
                        for kv in range(2):
                            rows = slice(64 * kv, 64 * kv + 64)
                            dve.wait_ge(s_kh, 4 * layer + 2 * kv + 2)
                            for half in range(2):
                                signal(dve.tensor_tensor(kl[64 * half:64 * half + 64, kv], kt[rows],
                                                         kh[rows, kv].bitcast(F32), ALU.subtract), s_kl)
                    m = att_pair_at(layer, n, tick, 1)
                    if m is not None:
                        b, j, _ = ATT_B[layer][2 * m]
                        MM = ATT_Q0[layer] // 2 + m
                        nq = N_META if b == 0 else P
                        for kv in range(2):
                            rows, other = slice(64 * kv, 64 * kv + 64), slice(64 - 64 * kv, 128 - 64 * kv)
                            dve.wait_ge(s_qh, 2 * MM + kv + 1)
                            signal(dve.tensor_tensor(qs[MM % 2][other, 4 * kv:4 * kv + 4, 0:nq],
                                                     y[rows, 4 + 4 * j:8 + 4 * j, blk(b)],
                                                     qs[MM % 2][rows, 4 * kv:4 * kv + 4, 0:nq].bitcast(F32),
                                                     ALU.subtract), s_ql)
                    at = att_at(layer, n, tick, 8)
                    if at and at[1] == 0:
                        att_meta(layer, at[0])
                    at = att_at(layer, n, tick, 0)
                    if at:
                        att_mask_max(layer, *at)
                    at = att_at(layer, n, tick, 10)
                    if at and at[1] == 0:
                        att_normalise(layer, at[0])
                    at = att_at(layer, n, tick, 11)
                    if at and at[1] == 0 and ATT_B[layer][at[0]][2] == 1:
                        att_out(layer, at[0])
                    h, r = hgrn_at(n, tick)
                    H = 4 * layer + h
                    if r == 1:
                        hgrn_prepare(layer, h)
                    if H_LEVEL <= r < H_LEVEL + 24 and (r - H_LEVEL) % 3 == 0:
                        hgrn_level_out(layer, H, (r - H_LEVEL) // 3)
                    if r == H_STATE:
                        hgrn_states(H)
                    if r == H_OUT:
                        hgrn_take_out(H)
                    if r == H_NORM:
                        hgrn_norm(layer, H)
            take_out(NTOT - 1)


def columns():
    sizes = (HA * P, HA * P, HA * P, HA * P, HB * DH, 2 * DH, 2 * DH, HB * DH, NG * P, NG * P)
    at = np.concatenate([[0], np.cumsum(sizes)])
    qa, fa, ia, ga, qb, kb, vb, gb, uc, gc = (int(a) for a in at[:-1])

    def pair(start, i):
        return np.concatenate([start + DH * i + np.arange(DH), start + DH * (i + GRP) + np.arange(DH)])

    def run(start, i):
        return start + P * i + np.arange(P)

    cols = []
    for kind, i in IN_CHUNKS:
        if kind == "gate":
            cols.append(run(ga, i) if i < 4 else pair(gb, i - 4) if i < 12 else run(gc, i - 12))
        else:
            cols.append({"k": lambda: run(kb, 0), "v": lambda: run(vb, 0), "q": lambda: pair(qb, i),
                         "u": lambda: run(uc, i), "hf": lambda: run(fa, i), "hq": lambda: run(qa, i),
                         "hi": lambda: run(ia, i)}[kind]())
    rows = [run(0, i) if i < 4 else pair(HA * P, i - 4) if i < 12 else run(0, i) for i in GATES]
    return np.concatenate(cols), np.concatenate(rows)


def constants():
    f = np.float32
    eye, ones = np.eye(P, dtype=f), np.ones((P, P), f)
    bones = np.kron(np.eye(2, dtype=f), np.ones((DH, DH), f))
    q, k = np.arange(P)[:, None], np.arange(P)[None, :]
    mask = np.zeros((P, 272), f)
    mask[:, 0:P] = np.where(k > q, 0.0, NEG)
    mask[:, P:2 * P] = np.where(k <= q, 0.0, NEG)
    recips = np.stack([1.0 / np.minimum(np.arange(PAD) + 1, w) for w in WINDOWS]).astype(f)
    recips = np.broadcast_to(recips.reshape(1, -1), (P, NG * PAD))
    c_f32 = np.ascontiguousarray(np.concatenate([eye, ones, bones, mask, recips], axis=1))
    inv = np.power(f(10000.0), -np.arange(DH // 2, dtype=f) * f(2.0) / f(DH)).astype(f)
    ang = (np.arange(T, dtype=f)[None, :] * inv[:, None]).astype(f)
    cos, sin = np.cos(ang).astype(f), np.sin(ang).astype(f)
    c_rope = np.ascontiguousarray(np.stack([np.concatenate([cos] * 4), np.concatenate([-sin, sin] * 2)], axis=1))
    lm = np.zeros((P, len(LEVELS), 64), f)
    for l, s in enumerate(LEVELS):
        i = np.arange(64)
        g = i // s
        j = np.arange(P)[:, None]
        m = (j // (2 * s) == g[None, :]) & (j % (2 * s) < s)
        lm[:, l] = m
    return c_rope, c_f32, np.ascontiguousarray(lm.reshape(P, -1))


def kernel(**inputs):
    import concourse.bacc as bacc
    from concourse.bass_utils import run_bass_kernel_spmd

    a = {k: np.asarray(v) for k, v in inputs.items()}
    cols, rows = columns()
    xT = np.concatenate([a["meta_tokens"], a["x"][0]], axis=0).T.reshape(KC, P, T).transpose(1, 0, 2)
    w_in = a["w_in"].reshape(DEPTH, KC, P, -1)[..., cols].reshape(DEPTH, KC, P, N_IN, P)
    w_in = w_in.transpose(0, 3, 2, 1, 4).reshape(DEPTH, N_IN, P, KC * P)
    w_out = a["w_out"][:, rows].reshape(DEPTH, KC, P, KC, P).transpose(0, 3, 2, 1, 4).reshape(DEPTH, KC, P, KC * P)

    prm = []
    for layer in range(DEPTH):
        def col(v):
            return v.reshape(-1, P).T

        def twice(v):
            return np.concatenate([v, v])[:, None]

        qg, kg = a["q_norm_g"][layer], a["k_norm_g"][layer]
        half = DH // 2
        swap = np.concatenate([np.arange(half, DH), np.arange(half)])
        prm.append(np.concatenate([
            col(a["norm_g"][layer]), twice(qg), twice(qg[swap]), twice(kg), twice(kg[swap]),
            a["hgrn_norm_g"][layer][:, None], col(a["pool_scale"][layer]),
            col(a["lb_logits"][0]), col(a["lb_logits"][1]),
            np.broadcast_to(a["attn_sinks"][layer][None, :], (P, HB))], axis=1))
    prm = np.stack(prm, axis=1)
    pool_w = a["pool_w"].transpose(2, 0, 1, 3).reshape(P, DEPTH, NG * P)
    c_rope, c_f32, c_mask = constants()

    nc = bacc.Bacc("TRN2", target_bir_lowering=False, num_devices=1)
    arrays, args = {}, []
    for name, v in (("xT", xT), ("w_in", w_in), ("w_out", w_out), ("prm", prm), ("pool_w", pool_w),
                    ("c_rope", c_rope), ("c_f32", c_f32), ("c_mask", c_mask)):
        v = np.ascontiguousarray(v)
        arrays[f"in_{name}"] = v
        args.append(nc.dram_tensor(f"in_{name}", v.shape, mybir.dt.from_np(v.dtype), kind="ExternalInput").ap())
    outT = nc.dram_tensor("out_0", [KC, P, SEQ], F32, kind="ExternalOutput").ap()
    h1T = nc.dram_tensor("h1T", [KC, P, T], F32, kind="Internal").ap()
    build(nc, *args, outT, h1T)
    r = run_bass_kernel_spmd(nc, [arrays], core_ids=[0])
    got = r.results[0]["out_0"]
    return np.ascontiguousarray(got.reshape(D_MODEL, SEQ).T)[None]
```

```python
from contextlib import ExitStack

import numpy as np

import concourse.bass as bass
from concourse import mybir

F32 = mybir.dt.float32
F32R = mybir.dt.float32r
U8 = mybir.dt.uint8
ACT = mybir.ActivationFunctionType
ALU = mybir.AluOpType

P = 128
DEPTH = 2
D_MODEL = 2048
N_META = 16
SEQ = 512
T = N_META + SEQ
KC = D_MODEL // P
HA = 4
HB = 16
DH = 64
GRP = 8
NG = 4
WINDOWS = (2, 4, 8, 16)
NBLK = SEQ // P
EPS = 1e-6
LOG_FLOOR = 1e-30
NEG = -1e30
PAD = 16

IN_CHUNKS = ([("v", 0), ("k", 0)] + [("q", i) for i in range(8)] + [("u", g) for g in range(NG)]
             + [("gate", 12 + g) for g in range(NG)]
             + [(kind, h) for h in range(HA) for kind in ("hf", "hq", "hi")]
             + [("gate", m) for m in (8, 9, 10, 11, 4, 5, 6, 7, 0, 1, 2, 3)])
N_IN = len(IN_CHUNKS)
CHUNKS = IN_CHUNKS + [("out", c) for c in range(KC)]
NC = len(CHUNKS)
NTOT = DEPTH * NC
GATES = [m for kind, m in IN_CHUNKS if kind == "gate"]
TICKS = KC
HI_TICKS = (2, 5, 8, 11)

MINI = {1: ("rms", 0)}
MINI.update({2 + i: ("rope", i) for i in range(9)})
MINI.update({11 + g: ("pool", g) for g in range(NG)})
MINI.update({23 + 3 * h: ("hnorm", h) for h in range(HA)})
MINI_SLOTS = sorted(MINI)
NORM_SLOTS = [n for n in MINI_SLOTS if MINI[n][0] != "pool"]
MINI_TICK, RMS_TICK = 8, 11


def mini_tick(n):
    return RMS_TICK if MINI[n][0] == "rms" else MINI_TICK


EARLY_SQUARES = 8
ROPE_CHUNKS = list(range(1, 10))
NROPE = len(ROPE_CHUNKS)
TANH_CHUNKS = [n for n, (kind, _) in enumerate(IN_CHUNKS) if kind in ("gate", "hq")]

C_NORM, C_QG, C_QGS, C_KG, C_KGS, C_HG, C_PS, C_LB, C_SINK, NPRM = 0, 16, 17, 18, 19, 20, 21, 25, 33, 49

ATT_SLOT, ATT_TICK, ATT_LEAD = 11, 2, 4
K_SPLIT_SLOTS, K_SPLIT_TICK = (6, 8), 7
EXP_LAG, PAIR_LAG, META_LAG, VALUE_LAG, OUT_LAG = 4, 6, 9, 11, 13


def att_job(n, tick):
    at = (n - ATT_SLOT) * TICKS + tick - ATT_TICK
    if at < 0 or (at and at * 5 // 8 == (at - 1) * 5 // 8):
        return None
    return at * 5 // 8


def att_batches(layer):
    first = 0 if layer == 0 else 1
    return [(b, j, kv) for b in range(first, NBLK + 1) for j in range(2) for kv in range(2)]


ATT_B = [att_batches(l) for l in range(DEPTH)]
ATT_Q0 = [0, len(ATT_B[0])]


def pairs_before(layer, q):
    return 2 * (sum(b > 0 for b, _, _ in ATT_B[0]) * layer + sum(b > 0 for b, _, _ in ATT_B[layer][:q]))


def hgrn_at(n, tick):
    h, r = divmod((n - 21) * TICKS + tick, 3 * TICKS)
    return (h, r) if 0 <= h < HA else (0, -1)


H_V_T, H_LEVEL, H_K_T, H_INC, H_STATE, H_OUT, H_SQ, H_NORM = 3, 4, 29, 31, 32, 34, 36, 46


def span(layer, n):
    kind = CHUNKS[n][0]
    return (N_META, SEQ // 2) if layer == DEPTH - 1 and kind in ("q", "gate", "out") else (0, T // 2)


AT_META, AT_CUR, BAND = P, P + N_META, 2 * P + N_META
KB = N_META + P


def band(b):
    return slice(AT_META if b < 2 else 0, AT_CUR if b == 0 else BAND)


def blk(b):
    return slice(0, N_META) if b == 0 else slice(N_META + P * (b - 1), N_META + P * b)


LEVELS = [1, 2, 4, 8, 16, 32, 64]
TAIL = T - 4 * P


def level_cols(s):
    return T if 2 * s <= TAIL else 4 * P


def build(nc, xT, w_in, w_out, prm, pool_w, c_rope, c_f32, c_mask, outT, h1T):
    ctx = ExitStack()
    with ctx:
        top = [0]
        base = -(-nc.sbuf_base // 64) * 64

        def place(name, shape, dt, at=None):
            size = int(np.prod(shape[1:])) * (1 if dt == U8 else 4)
            size = -(-size // 32) * 32
            if at is None:
                at = base + top[0]
                top[0] += size
                assert at + size <= nc.sbuf_usable_end, (name, at + size, nc.sbuf_usable_end)
            return nc.alloc_sbuf_tensor_at(name, shape, dt, offset=at), at + size

        U = T * 4
        xh, _ = place("x_hi", [P, KC, T], F32R)
        xl, _ = place("x_lo", [P, KC, T], F32R)
        mh_at = base + top[0]
        mh, _ = place("mixed_hi", [P, KC, T], F32R)
        ml_at = base + top[0]
        ml, _ = place("mixed_lo", [P, KC, T], F32R)
        wst, _ = place("w_stage", [P, 2, KC, P], F32)
        wh, _ = place("w_hi", [P, 2, KC, P], F32R)
        wl, _ = place("w_lo", [P, 2, KC, P], F32R)
        rstd, _ = place("rstd", [P, T], F32)
        prm_sb, _ = place("prm_sb", [P, DEPTH, NPRM], F32)
        pw_sb, _ = place("pool_w_sb", [P, DEPTH, NG, P], F32)
        cst, _ = place("cst", [P, P + BAND + NG * PAD], F32)
        sums, _ = place("ones", [P, 2, P], F32R)
        lmask, _ = place("level_mask", [P, len(LEVELS), 4, 64], U8)
        cst2, _ = place("cst2", [P, 2 * P + len(LEVELS) * 64], F32, ml_at)
        epsc, _ = place("eps_col", [P, 1], F32)
        coef, _ = place("hgrn_coef", [P, DEPTH, 4, HA], F32)
        lbt, _ = place("lb_tmp", [P, 8, HA], F32)
        stat, _ = place("att_stat", [P, 5, 4, 4], F32)
        z, _ = place("z", [P, 2, PAD + T], F32)
        ta, _ = place("ta", [P, PAD + T], F32)
        tb, _ = place("tb", [P, PAD + T], F32)
        th_at = base + top[0]
        th, _ = place("h_tanh", [P, T], F32)
        vt_at = base + top[0]
        vt, _ = place("h_vt", [P, T], F32)
        vh, _ = place("h_v", [P, 5, P], F32)
        pmt, _ = place("a_pmt", [P, P], F32)
        pmc, _ = place("a_pmeta", [P, 2, 4, N_META], F32)
        sqh, _ = place("square_hi", [P, T], F32R, vt_at)
        sql, _ = place("square_lo", [P, T], F32R, vt_at + T * 4)
        kt, _ = place("a_kt", [P, T], F32, th_at)
        qs = [place("a_q_stack0", [P, 8, P], F32R, vt_at)[0], place("a_q_stack1", [P, 8, P], F32R, mh_at)[0]]
        res = [place("res0", [P, T], F32, th_at)[0], place("res1", [P, T], F32, vt_at)[0]]

        y, _ = place("y", [P, KC, T], F32, ml_at)
        pts, a1 = place("a_pt", [P, 2, 2, 2, P], F32, ml_at)
        vm, a1 = place("a_vmeta", [P, 2, 4, DH], F32, a1)
        on, a1 = place("a_on", [P, 4, 2, DH], F32, a1)
        assert a1 <= ml_at + 4 * U
        kh, a2 = place("a_k_hi", [P, 2, NBLK, KB], F32R, mh_at + 2 * U)
        kl, a2 = place("a_k_lo", [P, 2, NBLK, KB], F32R, a2)
        vb, a2 = place("a_v", [P, NBLK + 1, P], F32, a2)
        pr, a2 = place("a_p", [P, 2, 4, BAND], F32, a2)
        assert a2 <= mh_at + 12 * U
        rope, a3 = place("rope", [P, 2, T], F32, mh_at)
        hf, a3 = place("h_f", [P, T], F32, mh_at)
        hk, a3 = place("h_k", [P, T], F32, a3)
        hq, a3 = place("h_q", [P, T], F32, a3)
        hp, a3 = place("h_qp", [P, T], F32, a3)
        tt, a3 = place("h_tot", [P, T], F32, a3)
        am, a3 = place("h_att", [P, 4, P], F32, a3)
        amt, a3 = place("h_att_tail", [P, TAIL], F32, a3)
        kn, a3 = place("h_kn", [P, 4, P], F32, a3)
        st, a3 = place("h_state", [P, 4, P], F32, a3)
        assert a3 <= mh_at + 8 * U
        hsqh, a4 = place("h_square_hi", [P, T], F32R, mh_at)
        hsql, a4 = place("h_square_lo", [P, T], F32R, a4)
        xin, _ = place("x_in", [P, KC, T], F32, mh_at)

        eye, ones, bones = cst[:, 0:P], sums[:, 0], sums[:, 1]
        lmask_f = cst2[:, 2 * P:].rearrange("p (l i) -> p l i", i=64)
        amask = cst[:, P:P + BAND]
        recips = cst[:, P + BAND:P + BAND + NG * PAD].rearrange("p (g t) -> p g t", g=NG)
        st_mx, st_neg, st_den, st_es, st_rd = (stat[:, i] for i in range(5))

        G = ctx.enter_context(nc.psum_tensor("ps_gemm", [P, 2, 2, 512], F32))
        M = ctx.enter_context(nc.psum_tensor("ps_mix", [P, 4, 512], F32))

        def sem(name):
            return ctx.enter_context(nc.semaphore(name))

        s_prm, s_prm0, s_rope = sem("const_in"), sem("prm_in"), sem("rope_in")
        s_x = [sem(f"x_in{q}") for q in range(4)]
        s_w = [sem("w_in0"), sem("w_in1")]
        s_wfirst = sem("w_in_first_quarter")
        s_whi, s_wlo, s_gemm, s_z = sem("w_hi_done"), sem("w_lo_done"), sem("gemm_done"), sem("z_done")
        s_mini, s_pevac = sem("mini_done"), sem("pool_evac")
        s_sqh, s_sql = sem("square_hi_done"), sem("square_lo_done")
        s_swap2 = sem("swap_done_vector")
        s_sq, s_swap, s_ln, s_rt, s_ropeo = (sem("square_done"), sem("swap_done"), sem("log_done"),
                                             sem("rsqrt_done"), sem("rope_done"))
        s_kh, s_kl, s_qh, s_ql = sem("a_k_hi_done"), sem("a_k_lo_done"), sem("a_q_hi_done"), sem("a_q_lo_done")
        s_amt, s_ame = sem("a_pmeta_ps"), sem("a_pmeta_sb")
        s_th, s_thf, s_prod, s_mhi, s_mlo = (sem("tanh_done"), sem("tanh_f_done"), sem("prod_done"),
                                             sem("mixed_hi_done"), sem("mixed_lo_done"))
        s_pool = sem("pooled_done")
        s_avt, s_avb, s_avz, s_avm = sem("a_v_t"), sem("a_v_sb"), sem("a_vmeta_zero"), sem("a_vmeta_in")
        s_asc, s_amx, s_aneg, s_aex, s_aes = (sem("a_scores"), sem("a_masked"), sem("a_negmax"),
                                              sem("a_exp"), sem("a_expsink"))
        s_apt, s_ape, s_apv, s_aoe, s_aot, s_aod, s_apm = (sem("a_pt_ps"), sem("a_pt_sb"), sem("a_pv"),
                                                    sem("a_o_norm"), sem("a_o_t"), sem("a_o_done"), sem("a_pmeta_c"))
        s_hq, s_hk, s_hvt, s_hve = sem("h_q_done"), sem("h_k_done"), sem("h_vt_ps"), sem("h_v_sb")
        s_hl, s_hu, s_hkt, s_hke = sem("h_level"), sem("h_update"), sem("h_kt_ps"), sem("h_kt_sb")
        s_hinc, s_hs, s_ho, s_hoe, s_hsq, s_hy = (sem("h_inc"), sem("h_states"), sem("h_o_ps"),
                                                  sem("h_o_sb"), sem("h_o_sq"), sem("h_y_done"))
        s_xhi, s_xsq, s_xlo, s_ss = sem("x_hi_done"), sem("x_sq_done"), sem("x_lo_done"), sem("x_ss_done")
        s_res = [sem("res_in0"), sem("res_in1")]
        s_sto = [sem("store0"), sem("store1")]
        s_lb, s_eps = sem("lb_step"), sem("eps_done")
        s_v = sem("vector_link")

        def parts(c0, w):
            return [(0, c0, 2 * w)] if 2 * w <= 512 else [(0, c0, w), (1, c0 + w, w)]

        def halves(ap, c0, w):
            return ap[:, c0:c0 + 2 * w] if 2 * w <= 512 else \
                ap[:, c0:c0 + 2 * w].rearrange("p (a t) -> p a t", a=2)

        def banks(slot, w):
            return G[:, slot, 0, 0:2 * w] if 2 * w <= 512 else G[:, slot, :, 0:w]

        def zs(par):
            return z[:, par, PAD:PAD + T]

        ta_, tb_ = ta[:, PAD:PAD + T], tb[:, PAD:PAD + T]

        def mini_no(layer, n):
            return layer * len(MINI_SLOTS) + MINI_SLOTS.index(n)

        def norm_no(layer, n):
            return layer * len(NORM_SLOTS) + NORM_SLOTS.index(n)

        def pool_no(layer, g):
            return layer * NG + g

        def tanh_no(layer, n):
            return layer * len(TANH_CHUNKS) + TANH_CHUNKS.index(n)

        def att_at(layer, n, tick, lag):
            job = att_job(n, tick)
            if job is None:
                return None
            q, i = divmod(job - ATT_LEAD - lag, 4)
            return (q, i) if 0 <= q < len(ATT_B[layer]) else None

        def store(sp, layer, n):
            c = n - N_IN
            N = NC * layer + n
            sp.wait_ge(s_z, N + 1)
            if layer < DEPTH - 1:
                sp.dma_start(h1T[c], zs(N % 2)).then_inc(s_sto[N % 2], 16)
            else:
                sp.dma_start(outT[c], z[:, N % 2, PAD + N_META:PAD + T]).then_inc(s_sto[N % 2], 16)

        def att_pair_at(layer, n, tick, job):
            now = att_job(n, tick)
            if now is None:
                return None
            m, r = divmod(now - job, 8)
            return m if r == 0 and 0 <= m < len(ATT_B[layer]) // 2 else None

        block = ctx.enter_context(nc.Block())

        @block.sync
        def _(sp):
            def load_w(N):
                if N >= 2:
                    sp.wait_ge(s_wlo, 4 * (N - 1))
                layer, n = divmod(N, NC)
                src = w_in[layer, n] if n < N_IN else w_out[layer, n - N_IN]
                sp.dma_start(wst[:, N % 2].rearrange("p k c -> p (k c)"), src).then_inc(s_w[N % 2], 16)

            def load_x(q):
                sp.dma_start(xin[:, 4 * q:4 * q + 4], xT[:, 4 * q:4 * q + 4]).then_inc(s_x[q], 16)

            sp.dma_start(prm_sb[:], prm).then_inc(s_prm0, 16)
            load_x(0)
            sp.dma_start(wst[:, 0, 0:4].rearrange("p k c -> p (k c)"), w_in[0, 0, :, 0:4 * P]).then_inc(s_wfirst, 16)
            load_x(1)
            sp.dma_start(wst[:, 0, 4:].rearrange("p k c -> p (k c)"), w_in[0, 0, :, 4 * P:]).then_inc(s_w[0], 16)
            load_x(2)
            load_x(3)
            load_w(1)
            sp.dma_start(pw_sb[:].rearrange("p l g c -> p l (g c)"), pool_w).then_inc(s_prm, 16)
            sp.dma_start(cst[:], c_f32).then_inc(s_prm, 16)
            sp.dma_start(cst2[:], c_mask).then_inc(s_prm, 16)
            for N in range(NTOT):
                layer, n = divmod(N, NC)
                if N + 2 < NTOT:
                    load_w(N + 2)
                if n == 0:
                    sp.wait_ge(s_xlo, 16)
                    sp.wait_ge(s_xsq, 16)
                    if layer:
                        sp.wait_ge(s_gemm, NC * layer)
                    sp.dma_start(rope[:], c_rope).then_inc(s_rope, 16)
                if n == 2:
                    sp.wait_ge(s_avb, 2 * layer + 2)
                    sp.wait_ge(s_avz, layer + 1)
                    for i in range(4):
                        sp.dma_start(vm[16 * i:16 * i + 16, :, i, :],
                                     vb[0:N_META, 0, :].rearrange("p (v d) -> p v d", v=2)).then_inc(s_avm, 16)
                if n >= N_IN - 1:
                    c = n - (N_IN - 1)
                    if c < KC:
                        if c < 2:
                            sp.wait_ge(s_hy, 4 * (layer + 1))
                        else:
                            sp.wait_ge(s_z, NC * layer + N_IN + c - 1)
                        if layer and c == 0:
                            for par in range(2):
                                sp.wait_ge(s_sto[par], 16 * (KC // 2))
                        src = xT[:, c] if layer == 0 else h1T[c]
                        sp.dma_start(res[c % 2][:], src).then_inc(s_res[c % 2], 16)
                if n > N_IN:
                    store(sp, layer, n - 1)
                if n == 0 and layer:
                    store(sp, layer - 1, NC - 1)
            store(sp, DEPTH - 1, NC - 1)
            for par in range(2):
                sp.wait_ge(s_sto[par], 16 * (KC // 2) * DEPTH)

        @block.gpsimd
        def _(pool):
            for layer in range(DEPTH):
                if layer:
                    pool.wait_ge(s_gemm, NC * layer)
                else:
                    pool.wait_ge(s_xlo, 16)
                    pool.wait_ge(s_xsq, 16)
                pool.memset(vm[:], 0.0).then_inc(s_avz, 1)
                for q in range(len(ATT_B[layer])):
                    Q = ATT_Q0[layer] + q
                    nq = N_META if ATT_B[layer][q][0] == 0 else P
                    if Q >= 2:
                        pool.wait_ge(s_amt, Q - 1)
                    for pair in range(2):
                        heads = slice(2 * pair, 2 * pair + 2)
                        pool.wait_ge(s_aex, 4 * Q + 2 * pair + 2)
                        pool.tensor_copy(pmc[0:nq, Q % 2, heads], pr[0:nq, Q % 2, heads, AT_META:AT_CUR])\
                            .then_inc(s_apm, 1)

        @block.scalar
        def _(act):
            def w_high(N, q):
                if N == 0 and q == 0:
                    act.wait_ge(s_wfirst, 16)
                elif q == (1 if N == 0 else 0):
                    act.wait_ge(s_w[N % 2], 16 * (N // 2 + 1))
                if N >= 2 and q == 0:
                    act.wait_ge(s_gemm, N - 1)
                act.activation(wh[:, N % 2, 4 * q:4 * q + 4], wst[:, N % 2, 4 * q:4 * q + 4], ACT.Copy)\
                   .then_inc(s_whi, 1)

            def x_high(layer, k, src):
                g = prm_sb[:, layer, C_NORM + k:C_NORM + k + 1]
                act.activation(xh[:, k], src, ACT.Copy, scale=g).then_inc(s_xhi, 1)

            def x_square(layer, k, src):
                if 16 * layer + k >= 2:
                    act.wait_ge(s_ss, 16 * layer + k - 1)
                act.activation((ta_, tb_)[k % 2], src, ACT.Square).then_inc(s_xsq, 1)

            act.wait_ge(s_prm0, 16)
            act.wait_ge(s_eps, 1)
            act.wait_ge(s_lb, 1)
            act.activation(lbt[:, 2:4], lbt[:, 0:2], ACT.Exp).then_inc(s_lb, 1)
            for k in range(KC):
                if k % 4 == 0:
                    act.wait_ge(s_x[k // 4], 16)
                x_high(0, k, xin[:, k])
                if 1 <= k <= EARLY_SQUARES:
                    x_square(0, k - 1, xin[:, k - 1])
                if k % 4 == 0:
                    w_high(0, k // 4)

            for N in range(NTOT):
                layer, n = divmod(N, NC)
                for tick in range(TICKS):
                    if tick == 0 and N:
                        pl, pn = divmod(N - 1, NC)
                        kind, idx = CHUNKS[pn]
                        zz = zs((N - 1) % 2)
                        c0, w = span(pl, pn)
                        cols = slice(c0, c0 + 2 * w)
                        if kind not in ("v", "u", "hi"):
                            act.wait_ge(s_z, N)
                        if kind in ("k", "q"):
                            R = NROPE * layer + ROPE_CHUNKS.index(pn)
                            if R:
                                act.wait_ge(s_ropeo, R)
                            act.activation(ta_[:, cols], zz[:, cols], ACT.Square).then_inc(s_sq, 1)
                            act.activation(sqh[:, cols], zz[:, cols], ACT.Square).then_inc(s_sqh, 1)
                            for quarter in range(2):
                                a, b = 32 * quarter, 32 * (quarter ^ 1)
                                act.activation(tb[a:a + 32, PAD + c0:PAD + c0 + 2 * w],
                                               z[b:b + 32, (N - 1) % 2, PAD + c0:PAD + c0 + 2 * w], ACT.Copy)\
                                   .then_inc(s_swap, 1)
                        elif kind in ("gate", "hq"):
                            act.activation(ta_[:, cols], zz[:, cols], ACT.Tanh, scale=0.5).then_inc(s_th, 1)
                        elif kind == "hf":
                            if 4 * pl + idx:
                                act.wait_ge(s_hk, 4 * pl + idx)
                            act.activation(th[:], zz, ACT.Tanh, scale=0.5).then_inc(s_thf, 1)
                        elif kind == "out" and pl < DEPTH - 1:
                            x_high(pl + 1, idx, zz)
                            x_square(pl + 1, idx, zz)
                    if tick in HI_TICKS and N + 1 < NTOT:
                        w_high(N + 1, HI_TICKS.index(tick))
                    if N == 0 and tick == 12:
                        for k in range(EARLY_SQUARES, KC):
                            x_square(0, k, xin[:, k])
                    if n == 1 and tick == RMS_TICK - 2:
                        act.wait_ge(s_ss, 16 * layer + 16)
                        act.activation(sqh[:], rstd[:], ACT.Copy).then_inc(s_sqh, 1)
                    if tick == 3 and N and CHUNKS[(N - 1) % NC][0] == "gate":
                        pl, pn = divmod(N - 1, NC)
                        gno = len(GATES) * pl + GATES.index(CHUNKS[pn][1])
                        c0, w = span(pl, pn)
                        act.wait_ge(s_prod, gno + 1)
                        m = CHUNKS[pn][1]
                        act.activation(mh[:, m, c0:c0 + 2 * w], zs((N - 1) % 2)[:, c0:c0 + 2 * w], ACT.Copy)\
                           .then_inc(s_mhi, 1)
                    if n in NORM_SLOTS and tick == mini_tick(n) + 1:
                        kind, idx = MINI[n]
                        no = norm_no(layer, n)
                        act.wait_ge(s_mini, mini_no(layer, n) + 1)
                        buf, size = {"rms": (rstd, D_MODEL), "rope": (ta_, DH), "hnorm": (tb_, P)}[kind]
                        c0, w = span(layer, n - 1) if kind == "rope" else (0, T // 2)
                        src = M[:, 0:2, 0:w] if kind == "rms" else banks((N + 1) % 2, w)
                        act.activation(halves(buf, c0, w), src, ACT.Ln, scale=1.0 / size,
                                       bias=epsc[:, 0:1]).then_inc(s_ln, 1)
                        act.wait_ge(s_ln, no + 1)
                        act.activation(buf[:, c0:c0 + 2 * w], buf[:, c0:c0 + 2 * w], ACT.Exp, scale=-0.5)\
                           .then_inc(s_rt, 1)
                    if n in K_SPLIT_SLOTS and tick == K_SPLIT_TICK:
                        kv = K_SPLIT_SLOTS.index(n)
                        src = kt[64 * kv:64 * kv + 64]
                        act.wait_ge(s_ropeo, NROPE * layer + 1)
                        for half in range(2):
                            dst = kh[64 * half:64 * half + 64, kv]
                            act.activation(dst[:, :, 0:N_META],
                                           src[:, 0:N_META].unsqueeze(1).broadcast_to([64, NBLK, N_META]),
                                           ACT.Copy).then_inc(s_kh, 1)
                            act.activation(dst[:, :, N_META:], src[:, N_META:].rearrange("p (b t) -> p b t", b=NBLK),
                                           ACT.Copy).then_inc(s_kh, 1)
                    m = att_pair_at(layer, n, tick, 0)
                    if m is not None:
                        b, j, _ = ATT_B[layer][2 * m]
                        MM = ATT_Q0[layer] // 2 + m
                        nq = N_META if b == 0 else P
                        act.wait_ge(s_ropeo, NROPE * (layer + 1))
                        if MM >= 2:
                            act.wait_ge(s_asc, 8 * (MM - 1))
                        for kv in range(2):
                            rows = slice(64 * kv, 64 * kv + 64)
                            act.activation(qs[MM % 2][rows, 4 * kv:4 * kv + 4, 0:nq],
                                           y[rows, 4 + 4 * j:8 + 4 * j, blk(b)], ACT.Copy).then_inc(s_qh, 1)
                    if n == 2 and tick == 2:
                        act.wait_ge(s_avt, layer + 1)
                        act.activation(vb[:, 1:NBLK + 1], M[:, 0].rearrange("p (b c) -> p b c", b=NBLK), ACT.Copy)\
                           .then_inc(s_avb, 1)
                        act.activation(vb[0:N_META, 0], M[0:N_META, 1, 0:P], ACT.Copy).then_inc(s_avb, 1)
                    at = att_at(layer, n, tick, EXP_LAG)
                    if at:
                        q, i = at
                        Q = ATT_Q0[layer] + q
                        b = ATT_B[layer][q][0]
                        nq = N_META if b == 0 else P
                        if i == 0:
                            act.wait_ge(s_aneg, Q + 1)
                            act.activation(st_es[0:nq, Q % 4], st_es[0:nq, Q % 4], ACT.Exp).then_inc(s_aes, 1)
                        act.activation(pr[0:nq, Q % 2, i, band(b)], pr[0:nq, Q % 2, i, band(b)], ACT.Exp,
                                       bias=st_neg[0:nq, Q % 4, i:i + 1],
                                       accum_out=st_den[0:nq, Q % 4, i:i + 1]).then_inc(s_aex, 1)
                    at = att_at(layer, n, tick, PAIR_LAG)
                    if at and at[1] % 2 == 1 and ATT_B[layer][at[0]][0]:
                        q, i = at
                        Q = ATT_Q0[layer] + q
                        first = 0 if ATT_B[layer][q][0] >= 2 else 1
                        act.wait_ge(s_apt, pairs_before(layer, q) + i // 2 + 1)
                        if Q:
                            act.wait_ge(s_apv, Q)
                        act.activation(pts[:, i // 2, :, first:2],
                                       M[:, 2].rearrange("p (i s q) -> p i s q", i=2, s=2)[:, :, first:2], ACT.Copy)\
                           .then_inc(s_ape, 1)
                    h, r = hgrn_at(n, tick)
                    H = 4 * layer + h
                    if r == H_V_T + 1:
                        act.wait_ge(s_hvt, H + 1)
                        if H:
                            act.wait_ge(s_ho, H)
                        act.activation(vh[:, 0:4], M[:, 3].rearrange("p (b c) -> p b c", b=4), ACT.Copy)\
                           .then_inc(s_hve, 1)
                        act.activation(vh[0:TAIL, 4], M[0:TAIL, 2, 0:P], ACT.Copy).then_inc(s_hve, 1)
                    if r == H_K_T + 1:
                        act.wait_ge(s_hkt, H + 1)
                        act.activation(kn[:], M[:, 0].rearrange("p (b c) -> p b c", b=4), ACT.Copy)\
                           .then_inc(s_hke, 1)
                    if r == H_SQ:
                        act.wait_ge(s_hoe, H + 1)
                        act.activation(tb_, y[:, H % 4], ACT.Square).then_inc(s_hsq, 1)
                        act.activation(hsqh[:], y[:, H % 4], ACT.Square).then_inc(s_sqh, 1)

        @block.tensor
        def _(pe):
            def mini(N, layer, n):
                kind, idx = MINI[n]
                no = mini_no(layer, n)
                g = M if kind == "rms" else G[:, (N + 1) % 2]
                c0, w = (0, T // 2)
                if kind == "rms":
                    if layer:
                        pe.wait_ge(s_hs, 4 * layer)
                else:
                    pe.wait_ge(s_z, N)
                if kind == "pool":
                    pe.wait_ge(s_pool, NG * layer + idx + 1)
                    lhs, parts_of = pw_sb[:, layer, idx], (ta_,)
                else:
                    if kind == "rope":
                        c0, w = span(layer, n - 1)
                    pe.wait_ge(s_sql, norm_no(layer, n) + 1)
                    lhs = bones if kind == "rope" else ones
                    parts_of = (hsqh, hsql) if kind == "hnorm" else (sqh, sql)
                for bank, c, size in parts(c0, w):
                    for i, rhs in enumerate(parts_of):
                        ins = pe.matmul(g[:, bank, 0:size], lhs, rhs[:, c:c + size],
                                        start=i == 0, stop=i == len(parts_of) - 1)
                ins.then_inc(s_mini, 1)

            def scores(layer, q, i):
                Q = ATT_Q0[layer] + q
                b, j, kv = ATT_B[layer][q]
                J = 4 * Q + i
                MM = Q // 2
                nq = N_META if b == 0 else P
                if i == 0 and kv == 0:
                    pe.wait_ge(s_ql, 2 * MM + 2)
                if q == 0 and i == 0:
                    pe.wait_ge(s_kl, 8 * layer + 8)
                    pe.wait_ge(s_avb, 2 * layer + 2)
                if J >= 2:
                    pe.wait_ge(s_amx, J - 1)
                qT = qs[MM % 2][:, 4 * kv + i, 0:nq]
                first = 0 if b < 2 else KB * (b - 2) + N_META
                size = band(b).stop - band(b).start
                for k_part in (kh, kl):
                    keys = k_part[:, kv].rearrange("p b t -> p (b t)")[:, first:first + size]
                    ins = pe.matmul(M[0:nq, J % 2, band(b)], qT, keys, start=k_part is kh, stop=k_part is kl)
                ins.then_inc(s_asc, 1)

            def probs_t(layer, q, pair):
                Q = ATT_Q0[layer] + q
                b = ATT_B[layer][q][0]
                no = pairs_before(layer, q) + pair
                pe.wait_ge(s_aex, 4 * Q + 2 * pair + 2)
                if no:
                    pe.wait_ge(s_ape, no)
                for i in range(2):
                    for s in range(0 if b >= 2 else 1, 2):
                        c, key = P * (2 * i + s), (0, AT_CUR)[s]
                        ins = pe.transpose(M[:, 2, c:c + P], pr[:, Q % 2, 2 * pair + i, key:key + P], eye)
                ins.then_inc(s_apt, 1)

            def probs_meta_t(layer, q):
                Q = ATT_Q0[layer] + q
                nq = N_META if ATT_B[layer][q][0] == 0 else P
                pe.wait_ge(s_apm, 2 * Q + 2)
                last = 4 * (ATT_Q0[layer] + len(ATT_B[layer]))
                pe.wait_ge(s_amx, min(4 * Q + META_LAG - 1, last))
                if Q:
                    pe.wait_ge(s_ame, Q)
                pe.transpose(M[0:64, 1, BAND:BAND + nq], pmc[0:nq, Q % 2].rearrange("p i k -> p (i k)"), eye[0:nq, 0:nq])\
                  .then_inc(s_amt, 1)

            def values(layer, q):
                Q = ATT_Q0[layer] + q
                b, j, kv = ATT_B[layer][q]
                nq = N_META if b == 0 else P
                pe.wait_ge(s_ame, Q + 1)
                if Q:
                    pe.wait_ge(s_aoe, Q)
                    pe.wait_ge(s_aod, Q // 2)
                if b:
                    pe.wait_ge(s_ape, pairs_before(layer, q + 1))
                if q == 0:
                    pe.wait_ge(s_avm, 64 * (layer + 1))
                o = M[0:nq, 3, 0:256]
                last = pe.matmul(o, pmt[0:64, 0:nq], vm[0:64, kv].rearrange("p i d -> p (i d)"),
                                 start=True, stop=b == 0)
                if b:
                    for i in range(4):
                        for s in range(0 if b >= 2 else 1, 2):
                            last = pe.matmul(o[:, DH * i:DH * i + DH], pts[:, i // 2, i % 2, s],
                                             vb[:, b - 1 + s, DH * kv:DH * kv + DH],
                                             start=False, stop=i == 3 and s == 1)
                last.then_inc(s_apv, 1)

            def outputs_t(layer, q):
                Q = ATT_Q0[layer] + q
                b = ATT_B[layer][q][0]
                nq = N_META if b == 0 else P
                pe.wait_ge(s_aoe, Q + 1)
                for i in range(4):
                    ins = pe.transpose(M[:, 3, P * i:P * i + nq], on[0:nq, i].rearrange("p v d -> p (v d)"),
                                       eye[0:nq, 0:nq])
                ins.then_inc(s_aot, 1)

            def hgrn_level(layer, H, l):
                bank = M[:, l % 2]
                pe.wait_ge(s_hk, H + 1)
                if l == 0:
                    if H == 4 * layer:
                        pe.wait_ge(s_amx, 4 * (ATT_Q0[layer] + len(ATT_B[layer])))
                        pe.wait_ge(s_ame, ATT_Q0[layer] + len(ATT_B[layer]))
                    if H:
                        pe.wait_ge(s_hs, H)
                else:
                    pe.wait_ge(s_hu, 8 * H + l)
                for b in range(4):
                    kcols = slice(P * b, P * b + P)
                    if l == 0:
                        ins = pe.matmul(bank[:, kcols], hk[:, kcols], hq[:, kcols], start=True, stop=True)
                    else:
                        s = LEVELS[l - 1]
                        rhs = hp[:, kcols].rearrange("p (g two s) -> p g two s", two=2, s=s)[:, :, 1]
                        ins = pe.matmul(bank[0:P - s, 64 * b:64 * b + 64], hk[:, P * b:P * b + P - s], rhs,
                                        start=True, stop=True)
                kcols = slice(4 * P, T)
                if l == 0:
                    ins = pe.matmul(M[0:TAIL, 1, 0:TAIL], hk[:, kcols], hq[:, kcols], start=True, stop=True)
                elif level_cols(LEVELS[l - 1]) == T:
                    s = LEVELS[l - 1]
                    rhs = hp[:, kcols].rearrange("p (g two s) -> p g two s", two=2, s=s)[:, :, 1]
                    ins = pe.matmul(bank[0:TAIL, 256:256 + TAIL // 2], hk[:, kcols], rhs, start=True, stop=True)
                ins.then_inc(s_hl, 1)

            def hgrn_v_t(H):
                pe.wait_ge(s_z, NC * (H // 4) + 21 + 3 * (H % 4))
                if H % 4:
                    pe.wait_ge(s_hoe, H)
                else:
                    pe.wait_ge(s_aod, (ATT_Q0[H // 4] + len(ATT_B[H // 4])) // 2)
                    pe.wait_ge(s_ape, pairs_before(H // 4, len(ATT_B[H // 4])))
                for b in range(4):
                    pe.transpose(M[:, 3, P * b:P * b + P], vt[:, P * b:P * b + P], eye)
                pe.transpose(M[0:TAIL, 2, 0:P], vt[:, 4 * P:T], eye).then_inc(s_hvt, 1)

            def hgrn_k_t(H):
                pe.wait_ge(s_hu, 8 * H + 8)
                for b in range(4):
                    ins = pe.transpose(M[:, 0, P * b:P * b + P], hk[:, P * b:P * b + P], eye)
                ins.then_inc(s_hkt, 1)

            def hgrn_increments(H):
                pe.wait_ge(s_hke, H + 1)
                pe.wait_ge(s_hve, 2 * H + 2)
                for b in range(4):
                    ins = pe.matmul(M[:, 1, P * b:P * b + P], kn[:, b], vh[:, b], start=True, stop=True)
                ins.then_inc(s_hinc, 1)

            def hgrn_out(H):
                pe.wait_ge(s_hs, H + 1)
                for b in range(5):
                    cols = slice(P * b, min(P * b + P, T))
                    o = M[:, 3, cols] if b < 4 else M[:, 2, 0:TAIL]
                    lhs = vh[:, b] if b < 4 else vh[0:TAIL, 4]
                    rhs = am[:, b] if b < 4 else amt[0:TAIL]
                    ins = pe.matmul(o, lhs, rhs, start=True, stop=b == 0)
                    if b:
                        ins = pe.matmul(o, st[:, b - 1], hp[:, cols], start=False, stop=True)
                ins.then_inc(s_ho, 1)

            for N in range(NTOT):
                layer, n = divmod(N, NC)
                g = G[:, N % 2]
                c0, w = span(layer, n)
                if N >= 2:
                    pe.wait_ge(s_z, N - 1)
                pl, pn = divmod(N - 1, NC)
                if N and pn in MINI:
                    if MINI[pn][0] == "pool":
                        pe.wait_ge(s_pevac, pool_no(pl, MINI[pn][1]) + 1)
                    elif MINI[pn][0] != "rms":
                        pe.wait_ge(s_ln, norm_no(pl, pn) + 1)
                for tick in range(TICKS):
                    k = tick if n < N_IN else GATES[tick]
                    if tick % 4 == 0:
                        pe.wait_ge(s_wlo, 4 * N + tick // 4 + 1)
                    if n == 0:
                        pe.wait_ge(s_xlo, 16 * layer + tick + 1)
                    if n == N_IN:
                        pe.wait_ge(s_mlo, len(GATES) * layer + tick + 1)
                    hi, lo = (xh, xl) if n < N_IN else (mh, ml)
                    passes = ((wh, hi), (wh, lo), (wl, hi))
                    for i, (ws, xs) in enumerate(passes):
                        for bank, c, size in parts(c0, w):
                            ins = pe.matmul(g[:, bank, 0:size], ws[:, N % 2, tick], xs[:, k, c:c + size],
                                            start=tick == 0 and i == 0, stop=tick == TICKS - 1 and i == 2)
                    if tick == TICKS - 1:
                        ins.then_inc(s_gemm, 1)
                    if N == 1 and tick == RMS_TICK:
                        pe.wait_ge(s_prm, 48)
                    if n in MINI and tick == mini_tick(n):
                        mini(N, layer, n)
                    if n == 2 and tick == 1:
                        pe.wait_ge(s_z, N - 1)
                        pe.wait_ge(s_ln, norm_no(layer, 1) + 1)
                        vz = zs(N % 2)
                        for b in range(NBLK):
                            pe.transpose(M[:, 0, P * b:P * b + P], vz[:, blk(b + 1)], eye)
                        pe.transpose(M[0:N_META, 1, 0:P], vz[:, 0:N_META], eye).then_inc(s_avt, 1)
                    at = att_at(layer, n, tick, META_LAG)
                    if at and at[1] == 0:
                        probs_meta_t(layer, at[0])
                    at = att_at(layer, n, tick, 0)
                    if at:
                        scores(layer, *at)
                    at = att_at(layer, n, tick, VALUE_LAG)
                    if at and at[1] == 0:
                        values(layer, at[0])
                    at = att_at(layer, n, tick, PAIR_LAG)
                    if at and at[1] % 2 == 1 and ATT_B[layer][at[0]][0]:
                        probs_t(layer, at[0], at[1] // 2)
                    at = att_at(layer, n, tick, OUT_LAG)
                    if at and at[1] == 0 and ATT_B[layer][at[0]][2] == 1:
                        outputs_t(layer, at[0])
                    h, r = hgrn_at(n, tick)
                    H = 4 * layer + h
                    if r == H_V_T:
                        hgrn_v_t(H)
                    if H_LEVEL <= r < H_LEVEL + 24 and (r - H_LEVEL) % 3 == 0:
                        hgrn_level(layer, H, (r - H_LEVEL) // 3)
                    if r == H_K_T:
                        hgrn_k_t(H)
                    if r == H_INC:
                        hgrn_increments(H)
                    if r == H_OUT:
                        hgrn_out(H)

        @block.vector
        def _(dve):
            links = [0]

            def link(ins):
                links[0] += 1
                ins.then_inc(s_v, 1)
                dve.wait_ge(s_v, links[0])

            counts = {}

            def signal(ins, s):
                counts[s.name] = counts[s.name] + 1 if s.name in counts else 1
                ins.then_inc(s, 1)
                dve.wait_ge(s, counts[s.name])

            def w_low(N, q):
                dve.wait_ge(s_whi, 4 * N + q + 1)
                part = (slice(None), N % 2, slice(4 * q, 4 * q + 4))
                dve.tensor_tensor(wl[part], wst[part], wh[part].bitcast(F32), ALU.subtract).then_inc(s_wlo, 1)

            def x_low(layer, k, src):
                g = prm_sb[:, layer, C_NORM + k:C_NORM + k + 1]
                dve.wait_ge(s_xhi, 16 * layer + k + 1)
                dve.scalar_tensor_tensor(xl[:, k], src, g, xh[:, k].bitcast(F32), ALU.mult, ALU.subtract)\
                   .then_inc(s_xlo, 1)

            def x_sum(layer, k):
                sq = (ta_, tb_)[k % 2]
                dve.wait_ge(s_xsq, 16 * layer + k + 1)
                if k == 0:
                    dve.tensor_copy(rstd[:], sq).then_inc(s_ss, 1)
                else:
                    dve.wait_ge(s_ss, 16 * layer + k)
                    dve.tensor_tensor(rstd[:], rstd[:], sq, ALU.add).then_inc(s_ss, 1)

            def square_low(no, lo, square, hi):
                dve.wait_ge(s_sqh, no + 1)
                signal(dve.tensor_tensor(lo, square, hi.bitcast(F32), ALU.subtract), s_sql)

            link(dve.memset(z[:, :, 0:PAD], 0.0))
            link(dve.memset(ta[:, 0:PAD], 0.0))
            link(dve.memset(tb[:, 0:PAD], 0.0))
            signal(dve.memset(epsc[:], EPS), s_eps)
            dve.wait_ge(s_prm0, 16)
            l0, l1 = prm_sb[:, 0, C_LB:C_LB + HA], prm_sb[:, 0, C_LB + HA:C_LB + 2 * HA]
            link(dve.tensor_tensor(lbt[:, 4], l0, l1, ALU.max))
            link(dve.tensor_tensor(lbt[:, 0], l0, lbt[:, 4], ALU.subtract))
            dve.tensor_tensor(lbt[:, 1], l1, lbt[:, 4], ALU.subtract).then_inc(s_lb, 1)
            for k in range(KC):
                x_low(0, k, xin[:, k])
                if k % 4 == 0:
                    w_low(0, k // 4)
                if 1 <= k <= EARLY_SQUARES:
                    x_sum(0, k - 1)
            def level_masks():
                for b in range(4):
                    link(dve.tensor_copy(lmask[:, :, b], lmask_f[:]))

            def hgrn_coefficients():
                dve.wait_ge(s_lb, 2)
                link(dve.tensor_tensor(lbt[:, 4], lbt[:, 2], lbt[:, 3], ALU.add))
                link(dve.reciprocal(lbt[:, 5], lbt[:, 4]))
                link(dve.tensor_tensor(lbt[:, 2], lbt[:, 2], lbt[:, 5], ALU.mult))
                link(dve.tensor_tensor(lbt[:, 3], lbt[:, 3], lbt[:, 5], ALU.mult))
                link(dve.tensor_tensor(lbt[:, 6], lbt[:, 2], lbt[:, 2], ALU.subtract))
                link(dve.tensor_tensor(lbt[:, 7], lbt[:, 2], lbt[:, 3], ALU.add))
                link(dve.tensor_tensor(lbt[:, 7], lbt[:, 7], lbt[:, 2], ALU.subtract))
                for layer in range(DEPTH):
                    lb, (a, b, na, ha) = lbt[:, 6 + layer], (coef[:, layer, i] for i in range(4))
                    link(dve.tensor_scalar(a, lb, -0.5, 0.5, ALU.mult, ALU.add))
                    link(dve.tensor_tensor(b, lb, a, ALU.add))
                    link(dve.tensor_scalar(na, a, -0.5, None, ALU.mult))
                    link(dve.tensor_scalar(ha, a, 0.5, None, ALU.mult))

            def take_out(N):
                layer, n = divmod(N, NC)
                kind, idx = CHUNKS[n]
                c0, w = span(layer, n)
                zz = zs(N % 2)
                src = banks(N % 2, w)
                dve.wait_ge(s_gemm, N + 1)
                if kind == "out":
                    dve.wait_ge(s_res[idx % 2], 16 * (KC // 2 * layer + idx // 2 + 1))
                    if KC * layer + idx >= 2:
                        dve.wait_ge(s_sto[N % 2], 16 * ((KC * layer + idx) // 2))
                    signal(dve.tensor_tensor(halves(zz, c0, w), src, halves(res[idx % 2], c0, w), ALU.add), s_z)
                    return
                if layer and n < 2:
                    dve.wait_ge(s_sto[N % 2], 16 * (KC // 2) * layer)
                if n == 0:
                    dve.wait_ge(s_rt, norm_no(layer, 1) + 1)
                dst = zz
                if kind == "hi":
                    dst = vt
                    if 4 * layer + idx:
                        dve.wait_ge(s_hvt, 4 * layer + idx)
                signal(dve.tensor_tensor(halves(dst, c0, w), src, halves(rstd, c0, w), ALU.mult), s_z)

            def rope_first(N):
                layer, n = divmod(N, NC)
                kind = CHUNKS[n][0]
                R = NROPE * layer + ROPE_CHUNKS.index(n)
                c0, w = span(layer, n)
                c = slice(c0, c0 + 2 * w)
                gcol = C_KG if kind == "k" else C_QG
                g, gs = (prm_sb[:, layer, gcol + i:gcol + i + 1] for i in range(2))
                zz = zs(N % 2)
                dve.wait_ge(s_rope, 16 * (layer + 1))
                dve.wait_ge(s_sq, R + 1)
                for quarter in range(2, 4):
                    a, b = 32 * quarter, 32 * (quarter ^ 1)
                    signal(dve.tensor_copy(tb[a:a + 32, PAD + c0:PAD + c0 + 2 * w],
                                           z[b:b + 32, N % 2, PAD + c0:PAD + c0 + 2 * w]), s_swap2)
                dve.wait_ge(s_swap, 2 * (R + 1))
                link(dve.scalar_tensor_tensor(tb_[:, c], tb_[:, c], gs, rope[:, 1, c], ALU.mult, ALU.mult))
                link(dve.scalar_tensor_tensor(zz[:, c], zz[:, c], g, rope[:, 0, c], ALU.mult, ALU.mult))
                link(dve.tensor_tensor(zz[:, c], zz[:, c], tb_[:, c], ALU.add))

            def rope_last(N):
                layer, n = divmod(N, NC)
                kind, idx = CHUNKS[n]
                c0, w = span(layer, n)
                c = slice(c0, c0 + 2 * w)
                dve.wait_ge(s_rt, norm_no(layer, n + 1) + 1)
                dst = kt[:, c] if kind == "k" else y[:, 4 + idx, c]
                R = NROPE * layer + ROPE_CHUNKS.index(n)
                signal(dve.tensor_tensor(dst, zs(N % 2)[:, c], ta_[:, c], ALU.mult), s_ropeo)

            def pool_out(N):
                layer, n = divmod(N, NC)
                idx = MINI[n][1]
                dve.wait_ge(s_mini, mini_no(layer, n) + 1)
                signal(dve.tensor_scalar(halves(y[:, 12 + idx], 0, T // 2), banks((N + 1) % 2, T // 2),
                                         prm_sb[:, layer, C_PS + idx:C_PS + idx + 1], None, ALU.mult), s_pevac)

            def pool_sum(g, j):
                return (tb if (WINDOWS[g].bit_length() - 2 - j) % 2 == 0 else ta)[:]

            def pooling(N, j):
                layer, n = divmod(N, NC)
                g, d = CHUNKS[n][1], 2 ** j
                if j == 0 and g == 0:
                    dve.wait_ge(s_ropeo, NROPE * (layer + 1))
                elif j == 0:
                    dve.wait_ge(s_pevac, pool_no(layer, g - 1) + 1)
                if d < WINDOWS[g]:
                    cur = pool_sum(g, j - 1) if j else z[:, N % 2]
                    link(dve.tensor_tensor(pool_sum(g, j)[:, PAD:], cur[:, PAD:], cur[:, PAD - d:PAD + T - d], ALU.add))

            def pooling_last(N):
                layer, n = divmod(N, NC)
                g = CHUNKS[n][1]
                u = z[:, N % 2]
                link(dve.tensor_tensor(ta[:, PAD:2 * PAD], tb[:, PAD:2 * PAD], recips[:, g], ALU.mult))
                link(dve.tensor_tensor(ta[:, PAD:2 * PAD], ta[:, PAD:2 * PAD], u[:, PAD:2 * PAD], ALU.subtract))
                signal(dve.scalar_tensor_tensor(ta[:, 2 * PAD:], tb[:, 2 * PAD:], 1.0 / WINDOWS[g], u[:, 2 * PAD:],
                                                ALU.mult, ALU.subtract), s_pool)

            def gate_product(N):
                layer, n = divmod(N, NC)
                m = CHUNKS[n][1]
                c0, w = span(layer, n)
                c = slice(c0, c0 + 2 * w)
                zz = zs(N % 2)
                dve.wait_ge(s_th, tanh_no(layer, n) + 1)
                link(dve.scalar_tensor_tensor(zz[:, c], ta_[:, c], 1.0, zz[:, c], ALU.add, ALU.mult))
                if m == 8:
                    dve.wait_ge(s_aod, (ATT_Q0[layer] + len(ATT_B[layer])) // 2)
                if m < HA:
                    dve.wait_ge(s_hy, 4 * layer + m + 1)
                signal(dve.scalar_tensor_tensor(zz[:, c], zz[:, c], 0.5, y[:, m, c], ALU.mult, ALU.mult), s_prod)

            def gate_low(N):
                layer, n = divmod(N, NC)
                m = CHUNKS[n][1]
                c0, w = span(layer, n)
                c = slice(c0, c0 + 2 * w)
                dve.wait_ge(s_mhi, len(GATES) * layer + GATES.index(m) + 1)
                signal(dve.tensor_tensor(ml[:, m, c], zs(N % 2)[:, c], mh[:, m, c].bitcast(F32), ALU.subtract), s_mlo)

            def att_mask_max(layer, q, i):
                Q = ATT_Q0[layer] + q
                b, j, kv = ATT_B[layer][q]
                J = 4 * Q + i
                nq = N_META if b == 0 else P
                head = GRP * kv + 4 * j + i
                sink = prm_sb[0:nq, layer, C_SINK + head:C_SINK + head + 1]
                mask = amask[0:nq, AT_CUR:AT_CUR + N_META] if b == 0 else amask[:, band(b)]
                dve.wait_ge(s_asc, J + 1)
                if Q >= 2 and i % 2 == 0:
                    pl, pq = (layer, q - 2) if q >= 2 else (layer - 1, len(ATT_B[layer - 1]) + q - 2)
                    if ATT_B[pl][pq][0]:
                        dve.wait_ge(s_apt, pairs_before(pl, pq) + i // 2 + 1)
                    dve.wait_ge(s_apm, 2 * (Q - 2) + i // 2 + 1)
                signal(dve.tensor_tensor_reduce(pr[0:nq, Q % 2, i, band(b)], M[0:nq, J % 2, band(b)], mask, DH ** -0.5,
                                         sink, ALU.add, ALU.max, st_mx[0:nq, Q % 4, i:i + 1]), s_amx)
                if i == 3:
                    dve.wait_ge(s_amx, J + 1)
                    link(dve.tensor_scalar(st_neg[0:nq, Q % 4], st_mx[0:nq, Q % 4], -1.0, None, ALU.mult))
                    sinks = prm_sb[0:nq, layer, C_SINK + head - 3:C_SINK + head + 1]
                    signal(dve.tensor_tensor(st_es[0:nq, Q % 4], sinks, st_mx[0:nq, Q % 4], ALU.subtract), s_aneg)

            def att_meta_out(layer, n, tick, q):
                Q = ATT_Q0[layer] + q
                nq = N_META if ATT_B[layer][q][0] == 0 else P
                now = att_at(layer, n, tick, 0)
                if now:
                    dve.wait_ge(s_asc, 4 * (ATT_Q0[layer] + now[0]) + now[1] + 1)
                dve.wait_ge(s_amt, Q + 1)
                if Q:
                    dve.wait_ge(s_apv, Q)
                signal(dve.tensor_copy(pmt[0:64, 0:nq], M[0:64, 1, BAND:BAND + nq]), s_ame)

            def att_normalise(layer, q):
                Q = ATT_Q0[layer] + q
                b, j, kv = ATT_B[layer][q]
                nq = N_META if b == 0 else P
                dve.wait_ge(s_aes, Q + 1)
                dve.wait_ge(s_aex, 4 * Q + 4)
                link(dve.tensor_tensor(st_rd[0:nq, Q % 4], st_den[0:nq, Q % 4], st_es[0:nq, Q % 4], ALU.add))
                link(dve.reciprocal(st_rd[0:nq, Q % 4], st_rd[0:nq, Q % 4]))
                dve.wait_ge(s_apv, Q + 1)
                rd = st_rd[0:nq, Q % 4].unsqueeze(2).broadcast_to([nq, 4, DH])
                signal(dve.tensor_tensor(on[0:nq, :, kv], M[0:nq, 3, 0:256]
                                  .rearrange("p (i d) -> p i d", i=4), rd, ALU.mult), s_aoe)

            def att_out(layer, q):
                Q = ATT_Q0[layer] + q
                b, j, kv = ATT_B[layer][q]
                nq = N_META if b == 0 else P
                dve.wait_ge(s_aot, Q // 2 + 1)
                signal(dve.tensor_copy(y[:, 4 + 4 * j:8 + 4 * j, blk(b)],
                                M[:, 3].rearrange("p (i q) -> p i q", i=4)[:, :, 0:nq]), s_aod)

            def hgrn_prepare(layer, h):
                H = 4 * layer + h
                a, b, na, ha = (coef[:, layer, i, h:h + 1] for i in range(4))
                dve.wait_ge(s_thf, H + 1)
                if H:
                    dve.wait_ge(s_ho, H)
                link(dve.tensor_scalar(hf[:], th[:], a, b, ALU.mult, ALU.add))
                link(dve.tensor_scalar(hf[:], hf[:], LOG_FLOOR, None, ALU.max))
                link(dve.tensor_scalar(hk[:], th[:], na, ha, ALU.mult, ALU.add))
                signal(dve.tensor_tensor(hp[:], hq[:], hf[:], ALU.mult), s_hk)
                dve.wait_ge(s_hk, H + 1)

            def hgrn_level_out(layer, H, l):
                dve.wait_ge(s_hl, 8 * H + l + 1)
                bank = M[:, l % 2]
                if l == 0:
                    e4 = eye.unsqueeze(1).broadcast_to([P, 4, P])
                    dve.tensor_tensor(am[:], bank.rearrange("p (b i) -> p b i", b=4), e4, ALU.mult)\
                       .then_inc(s_v, 1)
                    signal(dve.tensor_tensor(amt[0:TAIL], M[0:TAIL, 1, 0:TAIL], eye[0:TAIL, 0:TAIL], ALU.mult), s_hu)
                    links[0] += 1
                    dve.wait_ge(s_v, links[0])
                    dve.wait_ge(s_hu, 8 * H + 1)
                    return
                s = LEVELS[l - 1]
                cols = level_cols(s)
                ng = cols // (2 * s)
                amv = am[:].rearrange("p b i -> p (b i)").rearrange("p (g two s) -> p g two s", two=2, s=s)
                mask = lmask[:, l - 1].rearrange("p b i -> p (b i)").rearrange("p (g s) -> p g s", s=s)
                link(dve.copy_predicated(amv[0:P - s, :, 1], mask[0:P - s],
                                         bank[0:P - s, 0:256].rearrange("p (g s) -> p g s", s=s)))
                if cols == T:
                    atv = amt[0:TAIL].rearrange("p (g two s) -> p g two s", two=2, s=s)
                    link(dve.copy_predicated(atv[:, :, 1],
                                             lmask[0:TAIL, l - 1, 0, 0:TAIL // 2].rearrange("p (g s) -> p g s", s=s),
                                             bank[0:TAIL, 256:256 + TAIL // 2].rearrange("p (g s) -> p g s", s=s)))
                off = {1: None, 2: 0, 4: 264, 8: 396, 16: 462, 32: 495, 64: 511, 128: 519}
                cur = hf[:] if s == 1 else tt[:, off[s]:off[s] + 2 * ng]
                pair = cur[:, 0:2 * ng].rearrange("p (g two) -> p g two", two=2)
                qv = hp[:, 0:cols].rearrange("p (g two s) -> p g two s", two=2, s=s)
                kv = hk[:, 0:cols].rearrange("p (g two s) -> p g two s", two=2, s=s)
                link(dve.tensor_tensor(tt[:, off[2 * s]:off[2 * s] + ng], pair[:, :, 0], pair[:, :, 1], ALU.mult))
                link(dve.tensor_tensor(qv[:, :, 1], qv[:, :, 1],
                                       pair[:, :, 0].unsqueeze(2).broadcast_to([P, ng, s]), ALU.mult))
                signal(dve.tensor_tensor(kv[:, :, 0], kv[:, :, 0],
                                  pair[:, :, 1].unsqueeze(2).broadcast_to([P, ng, s]), ALU.mult), s_hu)
                dve.wait_ge(s_hu, 8 * H + l + 1)

            def hgrn_states(H):
                dve.wait_ge(s_hinc, H + 1)
                link(dve.tensor_copy(st[:, 0], M[:, 1, 0:P]))
                for b in range(1, 4):
                    ins = dve.scalar_tensor_tensor(st[:, b], st[:, b - 1], tt[:, 519 + b:520 + b],
                                                   M[:, 1, P * b:P * b + P], ALU.mult, ALU.add)
                    if b < 3:
                        link(ins)
                signal(ins, s_hs)

            def hgrn_take_out(H):
                dve.wait_ge(s_ho, H + 1)
                link(dve.tensor_copy(y[:, H % 4, 0:4 * P], M[:, 3]))
                signal(dve.tensor_copy(y[:, H % 4, 4 * P:T], M[:, 2, 0:TAIL]), s_hoe)

            def hgrn_norm(layer, H):
                dve.wait_ge(s_rt, norm_no(layer, 23 + 3 * (H % 4)) + 1)
                signal(dve.scalar_tensor_tensor(y[:, H % 4], y[:, H % 4], prm_sb[:, layer, C_HG:C_HG + 1], tb_,
                                         ALU.mult, ALU.mult), s_hy)

            for N in range(NTOT):
                layer, n = divmod(N, NC)
                pkind, pidx = CHUNKS[(N - 1) % NC] if N else ("", 0)
                for tick in range(TICKS):
                    if tick == (RMS_TICK + 1 if n == 1 else 0) and N:
                        take_out(N - 1)
                    if N == 0 and tick == 13:
                        for k in range(EARLY_SQUARES, KC):
                            x_sum(0, k)
                        dve.wait_ge(s_prm, 48)
                        link(dve.tensor_copy(sums[:].rearrange("p i c -> p (i c)"), cst2[:, 0:2 * P]))
                    if n == 1 and tick == RMS_TICK - 1:
                        dve.wait_ge(s_ss, 16 * layer + 16)
                        square_low(norm_no(layer, n), sql[:], rstd[:], sqh[:])
                    if tick == 2 and pkind in ("k", "q"):
                        pl, pn = divmod(N - 1, NC)
                        c0, w = span(pl, pn)
                        c = slice(c0, c0 + 2 * w)
                        square_low(norm_no(layer, n), sql[:, c], ta_[:, c], sqh[:, c])
                    if N == 4 and tick == 7:
                        level_masks()
                    if N == 3 and tick == 7:
                        hgrn_coefficients()
                    if tick == 1 and N >= 2 and CHUNKS[(N - 2) % NC][0] in ("k", "q"):
                        rope_last(N - 2)
                    if tick == 2 and pkind == "gate":
                        gate_product(N - 1)
                    if tick == 1:
                        if pkind == "hq":
                            pl, pn = divmod(N - 1, NC)
                            dve.wait_ge(s_th, tanh_no(pl, pn) + 1)
                            signal(dve.scalar_tensor_tensor(hq[:], ta_, 1.0, zs((N - 1) % 2), ALU.add, ALU.mult), s_hq)
                        if pkind == "out" and (N - 1) // NC < DEPTH - 1:
                            x_low((N - 1) // NC + 1, pidx, zs((N - 1) % 2))
                            x_sum((N - 1) // NC + 1, pidx)
                    if 1 <= tick <= 4 and pkind == "u":
                        pooling(N - 1, tick - 1)
                    if tick == 5 and pkind == "u":
                        pooling_last(N - 1)
                    if tick - 1 in HI_TICKS and N + 1 < NTOT:
                        w_low(N + 1, HI_TICKS.index(tick - 1))
                    if tick == 5 and pkind == "gate":
                        gate_low(N - 1)
                    if tick == 5 and pkind in ("k", "q"):
                        rope_first(N - 1)
                    if n in MINI and MINI[n][0] == "pool" and tick == mini_tick(n) + 1:
                        pool_out(N)
                    if n in K_SPLIT_SLOTS and tick == K_SPLIT_TICK + 3:
                        kv = K_SPLIT_SLOTS.index(n)
                        rows = slice(64 * kv, 64 * kv + 64)
                        src, hi = kt[rows], kh[rows, kv].bitcast(F32)
                        dve.wait_ge(s_kh, 8 * layer + 4 * kv + 4)
                        for half in range(2):
                            dst = kl[64 * half:64 * half + 64, kv]
                            signal(dve.tensor_tensor(dst[:, :, 0:N_META],
                                                     src[:, 0:N_META].unsqueeze(1).broadcast_to([64, NBLK, N_META]),
                                                     hi[:, :, 0:N_META], ALU.subtract), s_kl)
                            signal(dve.tensor_tensor(dst[:, :, N_META:],
                                                     src[:, N_META:].rearrange("p (b t) -> p b t", b=NBLK),
                                                     hi[:, :, N_META:], ALU.subtract), s_kl)
                    m = att_pair_at(layer, n, tick, 1)
                    if m is not None:
                        b, j, _ = ATT_B[layer][2 * m]
                        MM = ATT_Q0[layer] // 2 + m
                        nq = N_META if b == 0 else P
                        for kv in range(2):
                            rows, other = slice(64 * kv, 64 * kv + 64), slice(64 - 64 * kv, 128 - 64 * kv)
                            dve.wait_ge(s_qh, 2 * MM + kv + 1)
                            signal(dve.tensor_tensor(qs[MM % 2][other, 4 * kv:4 * kv + 4, 0:nq],
                                                     y[rows, 4 + 4 * j:8 + 4 * j, blk(b)],
                                                     qs[MM % 2][rows, 4 * kv:4 * kv + 4, 0:nq].bitcast(F32),
                                                     ALU.subtract), s_ql)
                    at = att_at(layer, n, tick, META_LAG)
                    if at and at[1] == 0:
                        att_meta_out(layer, n, tick, at[0])
                    at = att_at(layer, n, tick, 0)
                    if at:
                        att_mask_max(layer, *at)
                    at = att_at(layer, n, tick, VALUE_LAG)
                    if at and at[1] == 0:
                        att_normalise(layer, at[0])
                    at = att_at(layer, n, tick, OUT_LAG)
                    if at and at[1] == 0 and ATT_B[layer][at[0]][2] == 1:
                        att_out(layer, at[0])
                    h, r = hgrn_at(n, tick)
                    H = 4 * layer + h
                    if r == 1:
                        hgrn_prepare(layer, h)
                    if H_LEVEL <= r < H_LEVEL + 24 and (r - H_LEVEL) % 3 == 0:
                        hgrn_level_out(layer, H, (r - H_LEVEL) // 3)
                    if r == H_STATE:
                        hgrn_states(H)
                    if r == H_OUT:
                        hgrn_take_out(H)
                    if r == H_SQ + 1:
                        dve.wait_ge(s_hsq, H + 1)
                        square_low(norm_no(layer, n), hsql[:], tb_, hsqh[:])
                    if r == H_NORM:
                        hgrn_norm(layer, H)
            take_out(NTOT - 1)


def columns():
    sizes = (HA * P, HA * P, HA * P, HA * P, HB * DH, 2 * DH, 2 * DH, HB * DH, NG * P, NG * P)
    at = np.concatenate([[0], np.cumsum(sizes)])
    qa, fa, ia, ga, qb, kb, vb, gb, uc, gc = (int(a) for a in at[:-1])

    def pair(start, i):
        return np.concatenate([start + DH * i + np.arange(DH), start + DH * (i + GRP) + np.arange(DH)])

    def run(start, i):
        return start + P * i + np.arange(P)

    cols = []
    for kind, i in IN_CHUNKS:
        if kind == "gate":
            cols.append(run(ga, i) if i < 4 else pair(gb, i - 4) if i < 12 else run(gc, i - 12))
        else:
            cols.append({"k": lambda: run(kb, 0), "v": lambda: run(vb, 0), "q": lambda: pair(qb, i),
                         "u": lambda: run(uc, i), "hf": lambda: run(fa, i), "hq": lambda: run(qa, i),
                         "hi": lambda: run(ia, i)}[kind]())
    rows = [run(0, i) if i < 4 else pair(HA * P, i - 4) if i < 12 else run(0, i) for i in GATES]
    return np.concatenate(cols), np.concatenate(rows)


def constants():
    f = np.float32
    eye, ones = np.eye(P, dtype=f), np.ones((P, P), f)
    bones = np.kron(np.eye(2, dtype=f), np.ones((DH, DH), f))
    q, k = np.arange(P)[:, None], np.arange(P)[None, :]
    mask = np.zeros((P, BAND), f)
    mask[:, 0:P] = np.where(k > q, 0.0, NEG)
    mask[:, AT_CUR:] = np.where(k <= q, 0.0, NEG)
    recips = np.stack([1.0 / np.minimum(np.arange(PAD) + 1, w) for w in WINDOWS]).astype(f)
    recips = np.broadcast_to(recips.reshape(1, -1), (P, NG * PAD))
    c_f32 = np.ascontiguousarray(np.concatenate([eye, mask, recips], axis=1))
    inv = np.power(f(10000.0), -np.arange(DH // 2, dtype=f) * f(2.0) / f(DH)).astype(f)
    ang = (np.arange(T, dtype=f)[None, :] * inv[:, None]).astype(f)
    cos, sin = np.cos(ang).astype(f), np.sin(ang).astype(f)
    c_rope = np.ascontiguousarray(np.stack([np.concatenate([cos] * 4), np.concatenate([-sin, sin] * 2)], axis=1))
    lm = np.zeros((P, len(LEVELS), 64), f)
    for l, s in enumerate(LEVELS):
        i = np.arange(64)
        g = i // s
        j = np.arange(P)[:, None]
        m = (j // (2 * s) == g[None, :]) & (j % (2 * s) < s)
        lm[:, l] = m
    return c_rope, c_f32, np.ascontiguousarray(np.concatenate([ones, bones, lm.reshape(P, -1)], axis=1))


def kernel(**inputs):
    import concourse.bacc as bacc
    from concourse.bass_utils import run_bass_kernel_spmd

    a = {k: np.asarray(v) for k, v in inputs.items()}
    cols, rows = columns()
    xT = np.concatenate([a["meta_tokens"], a["x"][0]], axis=0).T.reshape(KC, P, T).transpose(1, 0, 2)
    w_in = a["w_in"].reshape(DEPTH, KC, P, -1)[..., cols].reshape(DEPTH, KC, P, N_IN, P)
    w_in = w_in.transpose(0, 3, 2, 1, 4).reshape(DEPTH, N_IN, P, KC * P)
    w_out = a["w_out"][:, rows].reshape(DEPTH, KC, P, KC, P).transpose(0, 3, 2, 1, 4).reshape(DEPTH, KC, P, KC * P)

    prm = []
    for layer in range(DEPTH):
        def col(v):
            return v.reshape(-1, P).T

        def twice(v):
            return np.concatenate([v, v])[:, None]

        qg, kg = a["q_norm_g"][layer], a["k_norm_g"][layer]
        half = DH // 2
        swap = np.concatenate([np.arange(half, DH), np.arange(half)])
        prm.append(np.concatenate([
            col(a["norm_g"][layer]), twice(qg), twice(qg[swap]), twice(kg), twice(kg[swap]),
            a["hgrn_norm_g"][layer][:, None], col(a["pool_scale"][layer]),
            col(a["lb_logits"][0]), col(a["lb_logits"][1]),
            np.broadcast_to(a["attn_sinks"][layer][None, :], (P, HB))], axis=1))
    prm = np.stack(prm, axis=1)
    pool_w = a["pool_w"].transpose(2, 0, 1, 3).reshape(P, DEPTH, NG * P)
    c_rope, c_f32, c_mask = constants()

    nc = bacc.Bacc("TRN2", target_bir_lowering=False, num_devices=1)
    arrays, args = {}, []
    for name, v in (("xT", xT), ("w_in", w_in), ("w_out", w_out), ("prm", prm), ("pool_w", pool_w),
                    ("c_rope", c_rope), ("c_f32", c_f32), ("c_mask", c_mask)):
        v = np.ascontiguousarray(v)
        arrays[f"in_{name}"] = v
        args.append(nc.dram_tensor(f"in_{name}", v.shape, mybir.dt.from_np(v.dtype), kind="ExternalInput").ap())
    outT = nc.dram_tensor("out_0", [KC, P, SEQ], F32, kind="ExternalOutput").ap()
    h1T = nc.dram_tensor("h1T", [KC, P, T], F32, kind="Internal").ap()
    build(nc, *args, outT, h1T)
    r = run_bass_kernel_spmd(nc, [arrays], core_ids=[0])
    got = r.results[0]["out_0"]
    return np.ascontiguousarray(got.reshape(D_MODEL, SEQ).T)[None]
```
